# Optimizing a Trainium2 kernel written in Bass

```python
import jax, jax.numpy as jnp
from jax import lax
import numpy as np

D_MODEL = 1024
BATCH = 1
SEQ = 512
DEPTH = 2

CHUNK = 64
EPS = 1e-6
ROPE_THETA = 10000.0
MASK_VALUE = -1e30

A_HEADS = 8
A_KV_HEADS = 2
A_HEAD_DIM = 64
A_WIDTH = A_HEADS * A_HEAD_DIM
A_KV_WIDTH = A_KV_HEADS * A_HEAD_DIM
WINDOW = 128
WINDOW_CHUNKS = WINDOW // CHUNK

B_GROUPS = 8
B_GROUP_DIM = 64
B_WIDTH = B_GROUPS * B_GROUP_DIM
B_BLOCK = 128

C_HEADS = 4
C_KEY_DIM = 128
C_VAL_DIM = 128
C_WIDTH = C_HEADS * C_KEY_DIM

N_BRANCH = 3
BRANCH_WIDTH = 512

IN_SIZES = (A_WIDTH, A_KV_WIDTH, A_KV_WIDTH, A_WIDTH,
            B_WIDTH, B_WIDTH, B_WIDTH,
            C_WIDTH, C_WIDTH, C_WIDTH, C_WIDTH,
            N_BRANCH * D_MODEL)
IN_WIDTH = sum(IN_SIZES)
SPLIT_IDX = tuple(int(i) for i in np.cumsum(IN_SIZES)[:-1])

kernel_name = "hybrid_swa_gmlp_hgrn2_block"

def rmsnorm(x, g):
    x32 = x.astype(jnp.float32)
    y = x32 * lax.rsqrt(jnp.mean(x32 * x32, axis=-1, keepdims=True) + EPS)
    return y.astype(x.dtype) * g

def layernorm(x, g, b):
    x32 = x.astype(jnp.float32)
    mu = jnp.mean(x32, axis=-1, keepdims=True)
    var = jnp.mean(jnp.square(x32 - mu), axis=-1, keepdims=True)
    return ((x32 - mu) * lax.rsqrt(var + EPS)).astype(x.dtype) * g + b

def rope(x, positions):
    hd = x.shape[-1]
    inv_freq = ROPE_THETA ** (-jnp.arange(0, hd, 2, dtype=jnp.float32) / hd)
    ang = positions.astype(jnp.float32)[..., None] * inv_freq
    cos = jnp.cos(ang)[:, :, None, :]
    sin = jnp.sin(ang)[:, :, None, :]
    x32 = x.astype(jnp.float32)
    x1, x2 = x32[..., : hd // 2], x32[..., hd // 2:]
    out = jnp.concatenate([x1 * cos - x2 * sin, x2 * cos + x1 * sin], axis=-1)
    return out.astype(x.dtype)

def sliding_window_attention(q, k, v, sinks):
    b_, s_ = q.shape[0], q.shape[1]
    nc = s_ // CHUNK
    rep = A_HEADS // A_KV_HEADS
    qc = q.reshape(b_, nc, CHUNK, A_KV_HEADS, rep, A_HEAD_DIM)
    pad = ((0, 0), ((WINDOW_CHUNKS - 1) * CHUNK, 0), (0, 0), (0, 0))
    kc = jnp.pad(k, pad).reshape(b_, nc + WINDOW_CHUNKS - 1, CHUNK, A_KV_HEADS, A_HEAD_DIM)
    vc = jnp.pad(v, pad).reshape(b_, nc + WINDOW_CHUNKS - 1, CHUNK, A_KV_HEADS, A_HEAD_DIM)
    kb = jnp.concatenate([kc[:, j:j + nc] for j in range(WINDOW_CHUNKS)], axis=2)
    vb = jnp.concatenate([vc[:, j:j + nc] for j in range(WINDOW_CHUNKS)], axis=2)
    key_chunk = (jnp.arange(nc)[:, None] - (WINDOW_CHUNKS - 1)
                 + jnp.arange(WINDOW)[None, :] // CHUNK)
    valid = key_chunk >= 0
    s = jnp.einsum('bnqgrd,bnkgd->bngrqk', qc, kb).astype(jnp.float32) * (A_HEAD_DIM ** -0.5)
    s = jnp.where(valid[None, :, None, None, None, :], s, MASK_VALUE)
    sink = jnp.broadcast_to(sinks.astype(jnp.float32).reshape(1, 1, A_KV_HEADS, rep, 1, 1),
                            s.shape[:-1] + (1,))
    p = jax.nn.softmax(jnp.concatenate([s, sink], axis=-1), axis=-1)[..., :-1]
    o = jnp.einsum('bngrqk,bnkgd->bnqgrd', p.astype(v.dtype), vb)
    return o.reshape(b_, s_, A_WIDTH)

def spatial_gating(u, v, w_s, b_s, ln_g, ln_b):
    b_, s_ = u.shape[0], u.shape[1]
    nb = s_ // B_BLOCK
    v = layernorm(v, ln_g, ln_b)
    vb = v.reshape(b_, nb, B_BLOCK, B_GROUPS, B_GROUP_DIM)
    pos_chunk = jnp.arange(B_BLOCK) // CHUNK
    mask = pos_chunk[None, :] <= pos_chunk[:, None]
    w = jnp.where(mask[None], w_s, jnp.zeros_like(w_s))
    sv = jnp.einsum('gts,bnsgc->bntgc', w, vb) + b_s.T[None, None, :, :, None]
    return u * sv.reshape(b_, s_, B_WIDTH)

def hgrn2_chunkwise(q, k, v, logf):
    b_, s_, h, dk = q.shape
    dv = v.shape[-1]
    nc = s_ // CHUNK

    def to_chunks(t):
        return t.astype(jnp.float32).reshape(b_, nc, CHUNK, h, t.shape[-1]).transpose(1, 0, 3, 2, 4)

    qs, ks, vs, gs = to_chunks(q), to_chunks(k), to_chunks(v), to_chunks(logf)
    causal = jnp.tril(jnp.ones((CHUNK, CHUNK), dtype=bool))[:, :, None]

    def step(state, inp):
        qc, kc, vc, gc = inp
        bcum = jnp.cumsum(gc, axis=2)
        diff = bcum[:, :, :, None, :] - bcum[:, :, None, :, :]
        decay = jnp.where(causal, jnp.exp(jnp.where(causal, diff, 0.0)), 0.0)
        attn = jnp.sum(qc[:, :, :, None, :] * kc[:, :, None, :, :] * decay, axis=-1)
        o = (jnp.einsum('bhts,bhse->bhte', attn, vc)
             + jnp.einsum('bhtd,bhde->bhte', qc * jnp.exp(bcum), state))
        blast = bcum[:, :, -1:, :]
        new_state = (jnp.exp(blast)[:, :, 0, :, None] * state
                     + jnp.einsum('bhsd,bhse->bhde', kc * jnp.exp(blast - bcum), vc))
        return new_state, o

    s0 = jnp.zeros((b_, h, dk, dv), jnp.float32)
    _, o = lax.scan(step, s0, (qs, ks, vs, gs))
    return o.transpose(1, 0, 3, 2, 4).reshape(b_, s_, h, dv)

def setup_inputs(seed: int = 0) -> dict:
    key = jax.random.key(seed)
    ks = jax.random.split(key, 16)
    f32 = jnp.float32
    x = jax.random.normal(ks[0], (BATCH, SEQ, D_MODEL), f32)
    offsets = jax.random.randint(ks[1], (BATCH, 1), 0, 1024, dtype=jnp.int32)
    positions = (offsets + jnp.arange(SEQ, dtype=jnp.int32)[None, :]).astype(jnp.int32)
    w_in = jax.random.normal(ks[2], (DEPTH, D_MODEL, IN_WIDTH), f32) * D_MODEL ** -0.5
    b_merge = jax.random.normal(ks[3], (DEPTH, N_BRANCH, D_MODEL), f32) * 0.1
    w_branch = jax.random.normal(ks[4], (DEPTH, N_BRANCH, BRANCH_WIDTH, D_MODEL), f32) * BRANCH_WIDTH ** -0.5
    w_out = jax.random.normal(ks[5], (DEPTH, D_MODEL, D_MODEL), f32) * (0.5 * D_MODEL ** -0.5)
    norm_g = 1.0 + 0.05 * jax.random.normal(ks[6], (DEPTH, D_MODEL), f32)
    final_g = 1.0 + 0.05 * jax.random.normal(ks[7], (D_MODEL,), f32)
    attn_sinks = 0.5 * jax.random.normal(ks[8], (DEPTH, A_HEADS), f32)
    sp_w = jax.random.normal(ks[9], (DEPTH, B_GROUPS, B_BLOCK, B_BLOCK), f32) * (0.5 * B_BLOCK ** -0.5)
    sp_b = 1.0 + 0.1 * jax.random.normal(ks[10], (DEPTH, B_GROUPS, B_BLOCK), f32)
    sp_ln_g = 1.0 + 0.05 * jax.random.normal(ks[11], (DEPTH, B_WIDTH), f32)
    sp_ln_b = 0.05 * jax.random.normal(ks[12], (DEPTH, B_WIDTH), f32)
    hgrn_lb = jax.random.normal(ks[13], (DEPTH, C_WIDTH), f32)
    hgrn_norm_g = 1.0 + 0.05 * jax.random.normal(ks[14], (DEPTH, C_WIDTH), f32)
    return {"x": x, "positions": positions, "w_in": w_in, "b_merge": b_merge,
            "w_branch": w_branch, "w_out": w_out, "norm_g": norm_g, "final_g": final_g,
            "attn_sinks": attn_sinks, "sp_w": sp_w, "sp_b": sp_b, "sp_ln_g": sp_ln_g,
            "sp_ln_b": sp_ln_b, "hgrn_lb": hgrn_lb, "hgrn_norm_g": hgrn_norm_g}

def reference(x, positions, w_in, b_merge, w_branch, w_out, norm_g, final_g,
              attn_sinks, sp_w, sp_b, sp_ln_g, sp_ln_b, hgrn_lb, hgrn_norm_g):
    b_, s_ = x.shape[0], x.shape[1]
    lb_soft = jax.nn.softmax(hgrn_lb.astype(jnp.float32), axis=0)
    lower_bounds = jnp.cumsum(lb_soft, axis=0) - lb_soft[0]
    for l in range(DEPTH):
        h = rmsnorm(x, norm_g[l])
        proj = h @ w_in[l]
        (a_q, a_k, a_v, a_gate, b_u, b_v, b_gate,
         c_q, c_f, c_i, c_gate, merge) = jnp.split(proj, SPLIT_IDX, axis=-1)

        qa = rope(a_q.reshape(b_, s_, A_HEADS, A_HEAD_DIM), positions)
        ka = rope(a_k.reshape(b_, s_, A_KV_HEADS, A_HEAD_DIM), positions)
        va = a_v.reshape(b_, s_, A_KV_HEADS, A_HEAD_DIM)
        out_a = sliding_window_attention(qa, ka, va, attn_sinks[l]) * jax.nn.silu(a_gate)

        out_b = spatial_gating(jax.nn.gelu(b_u), jax.nn.gelu(b_v), sp_w[l], sp_b[l],
                               sp_ln_g[l], sp_ln_b[l]) * jax.nn.silu(b_gate)

        lb = jnp.clip(lower_bounds[l], 0.0, 1.0).reshape(C_HEADS, C_KEY_DIM)
        fr = c_f.reshape(b_, s_, C_HEADS, C_KEY_DIM).astype(jnp.float32)
        f = lb + (1.0 - lb) * jax.nn.sigmoid(fr)
        logf = jnp.log(f)
        kk = 1.0 - f
        oc = hgrn2_chunkwise(c_q.reshape(b_, s_, C_HEADS, C_KEY_DIM), kk,
                             c_i.reshape(b_, s_, C_HEADS, C_VAL_DIM), logf)
        oc = rmsnorm(oc, hgrn_norm_g[l].reshape(C_HEADS, C_VAL_DIM)).astype(x.dtype)
        out_c = oc.reshape(b_, s_, C_WIDTH) * jax.nn.silu(c_gate)

        branches = jnp.stack([out_a, out_b, out_c], axis=2)
        gates = jax.nn.sigmoid(merge.reshape(b_, s_, N_BRANCH, D_MODEL) + b_merge[l])
        mixed = jnp.einsum('bsnc,ncd->bsnd', branches, w_branch[l])
        y = jnp.sum(gates * mixed, axis=2) @ w_out[l]
        x = x + y
    return rmsnorm(x, final_g)


_drawn_inputs = setup_inputs


def setup_inputs(seed=0):
    import zlib

    import numpy as np

    out = dict(_drawn_inputs(seed))
    spreads = {}
    factors = {'b_merge': 5.188,
     'attn_sinks': 62.35,
     'sp_b': 3.819,
     'sp_ln_g': 21.896,
     'sp_ln_b': 22.33,
     'hgrn_norm_g': 5.009}
    for name, (base, spread) in spreads.items():
        noise = np.random.default_rng([zlib.crc32(name.encode()), seed]).standard_normal(out[name].shape)
        drawn = base * np.exp(spread * noise) if base else spread * noise
        out[name] = __import__('jax').numpy.asarray(drawn.astype(out[name].dtype))
    for name, factor in factors.items():
        out[name] = (out[name] * factor).astype(out[name].dtype)
    return out
```

```python
from contextlib import ExitStack

import numpy as np
import concourse.bass as bass
from concourse import mybir

DEPTH, T, D = 2, 512, 1024
P = 128
KT = D // P
TB = T // P
A_HEADS, HD = 8, 64
EPS = 1e-6
ROPE_THETA = 10000.0
MASK_VALUE = -1e30
AQ, AK, AV, AG, BU, BV, BG, CQ, CF, CI, CG, MG = (
    int(v) for v in np.cumsum([0, 512, 128, 128, 512, 512, 512, 512, 512, 512, 512, 512]))
UC = 256
KB = 1024

UNITS = ([("q", 0), ("q", 1), ("k", 0), ("v", 0)]
         + [(k, p) for p in range(2) for k in ("cf", "cq", "ci")]
         + [("bv", 0), ("bv", 1), ("ag", 0), ("ag", 1), ("bu", 0), ("bu", 1)]
         + [("bg", 0), ("bg", 1), ("cg", 0), ("cg", 1)]
         + [(k, p * 3 + n) for p in range(4) for n in range(3) for k in ("merge", "mix")]
         + [("out", o) for o in range(4)])
NU = len(UNITS)
JOBS = [(u, t) for u in range(NU) for t in range(1 if UNITS[u][0] in ("k", "v") else 2)]
NJ = len(JOBS)
KIND = [UNITS[u][0] for u, _ in JOBS]
FIRST = {UNITS[u]: n for n, (u, t) in enumerate(JOBS) if t == 0}
JOBS_TO = [max(n for n, (v, _) in enumerate(JOBS) if v == u) + 1 for u in range(NU)]
BY_VECTOR = ("cf", "mix", "out")
EVAC_NO = []
for _k in KIND:
    _e = "v" if _k in BY_VECTOR else "a"
    EVAC_NO.append((_e, 1 + sum(e == _e for e, _ in EVAC_NO)))
SG_JOBS = [n for n in range(NJ) if KIND[n] in ("ag", "bu", "bg", "cg")]
GATE_JOBS = [n for n in SG_JOBS if KIND[n] != "bu"]
BRANCH = {"ag": 0, "bg": 1, "cg": 2}
LEVELS = 7
DIAG = (12, 24)
NJP = 3
WB, RB = 2, 3
assert NU % WB == 0 and NU % RB == 0


def constants():
    c = np.zeros((P, P + 64 * LEVELS + P + 8), np.float32)
    c[:, 0:P] = np.eye(P)
    for lev in range(LEVELS):
        s = 64 >> lev
        for i in range(P):
            if i % (2 * s) < s:
                b = i // (2 * s)
                c[i, P + 64 * lev + b * s:P + 64 * lev + (b + 1) * s] = 1.0
    o = P + 64 * LEVELS
    c[0, o:o + 64] = 1.0
    c[1, o + 64:o + 128] = 1.0
    freq = np.float32(ROPE_THETA) ** (-np.arange(0, HD, 2, dtype=np.float32) / np.float32(HD))
    c[:, o + P] = np.tile(freq, P // (HD // 2))
    c[:, o + P + 1] = np.where(np.arange(P) % HD < HD // 2, -2.0, 2.0)
    return c


def build(nc, x, positions, w_in, b_merge, w_branch, w_out, norm_g, final_g, attn_sinks, sp_w, sp_b,
          sp_ln_g, sp_ln_b, hgrn_lb, hgrn_norm_g, consts, out):
    f32, f32r, i32 = mybir.dt.float32, mybir.dt.float32r, mybir.dt.int32
    ALU = mybir.AluOpType
    ACT = mybir.ActivationFunctionType
    AX = mybir.AxisListType.X
    SCALE = HD ** -0.5
    NC_ = consts.shape[1]

    ctx = ExitStack()
    with ctx:
        base = [-(-nc.sbuf_base // 32) * 32]

        def region(kib):
            at = base[0]
            base[0] += int(kib * KB)
            return at

        def at(name, shape, offset, dt=f32):
            return nc.alloc_sbuf_tensor_at(name, shape, dt, offset=offset)

        XT = at("xT", [P, KT, T], region(16))
        HH = at("h_hi", [P, KT, T], r_hh := region(16), f32r)
        HL = at("h_lo", [P, KT, T], region(16), f32r)
        r_raw = region(8 * RB)
        RAW = at("w_raw", [P, RB, KT * UC], r_raw)
        WLO = at("w_lo", [P, RB, KT * UC], r_raw, f32r)
        WHI = at("w_hi", [P, WB, KT * UC], region(8 * WB), f32r)
        r_brh, r_brl = region(24), region(24)
        BRH = at("branch_hi", [P, 3, 4, T], r_brh, f32r)
        BRL = at("branch_lo", [P, 3, 4, T], r_brl, f32r)
        OX = at("branch_out", [P, 3, 4, T], r_brh)
        r_ob, r_oc3 = r_brh + 8 * KB, r_brh + 22 * KB
        SPW = at("sp_w_rows", [P, 8, P], r_ob)
        LNG = at("ln_g", [P, T], r_ob + 4 * KB)
        LNB = at("ln_b", [P, T], r_ob + 6 * KB)
        SPB = at("sp_b_rows", [2, 4, P], r_oc3)
        PR = at("probs", [P, 2, TB, P], r_brl)
        VA = at("v_a", [P, TB, P], r_brl + 4 * KB)
        KP = at("k_rot", [P, T], r_brl + 6 * KB)
        BC = [at(f"decay_cum{p}", [P, 2, T], r_brl + (8 + 8 * p) * KB) for p in range(2)]
        KK = [at(f"key_c{p}", [P, 2, T], r_brl + (12 + 8 * p) * KB) for p in range(2)]
        r_scr = region(40)
        YH = at("y_hi", [P, KT, T], r_scr, f32r)
        YL = at("y_lo", [P, KT, T], r_scr + 16 * KB, f32r)
        GM = at("merge_gate", [P, 2, 2, T], r_scr + 32 * KB)
        XTOK = at("x_tokens", [P, TB, D], r_scr)
        QP = at("q_rot", [P, 4, T], r_scr)
        GV = at("gelu_v", [P, TB, T], r_scr)
        PT = at("probsT", [P, 2, T], r_scr + 8 * KB)
        WT = at("sp_wT", [P, 8, P], r_scr + 8 * KB)
        QC = [at(f"query_c{p}", [P, 2, T], r_scr + (12 + 4 * p) * KB) for p in range(2)]
        VC = at("v_c", [P, TB, T], r_scr + 20 * KB)
        XL = [at(f"level_ops{b}", [P, 2 * T], r_scr + (28 + 4 * b) * KB) for b in range(2)]
        KHT = at("k_hatT", [P, 2, 3, P], r_scr + 36 * KB)
        VB = at("v_a_even", [P, TB, P], r_scr + 36 * KB)
        E = [at(f"decay{b}", [P, 2 * T], region(4)) for b in range(2)]
        SS = at("sum_sq", [P, T], r_e := base[0] - 8 * KB)
        RS = at("rstd", [P, T], r_e + 4 * KB)
        QS = at("q_halves_swapped", [P, 2, T], r_e)
        r_at = region(4)
        AT = at("attnT", [P, 2, T], r_at)
        R1 = at("rope_cos", [P, T], r_at)
        R2 = at("rope_sin", [P, T], r_at + 2 * KB)
        TP = at("product", [P, 2, T], r_at)
        ST = at("state", [P, 2, 3, P], region(3))
        r_sg = region(4)
        SG = at("gate", [P, 2, T], r_sg)
        QR = at("q_raw", [P, 2, T], r_sg)
        TT = at("full", [P, 2, T], region(4))
        CST = at("consts", [P, NC_], region(NC_ * 4 / KB))
        ONE = at("ones", [P, P], region(0.5))
        COS = at("cos", [P, T], region(2))
        SIN = at("sin", [P, T], region(2))
        base[0] = -(-base[0] // 32) * 32
        small = at("small", [P, 250], region(1000 / KB))
        assert DEPTH == 2
        assert base[0] <= nc.sbuf_usable_end, (base[0], nc.sbuf_usable_end)
        VL = small[:, 0:96].rearrange("p (l c) -> p l c", l=2)
        VC48 = small[:, 96:144]
        SK, NSK = small[:, 152:160], small[:, 160:168]
        MX = small[:, 168:172]
        NM = small[:, 172:180].rearrange("p (b t) -> p b t", b=2)
        SM = small[:, 180:188].rearrange("p (b t) -> p b t", b=2)
        ES = small[:, 188:196].rearrange("p (b t) -> p b t", b=2)
        DN = small[:, 196:200]
        RD = small[:, 200:204]
        BS = small[:, 204:228].rearrange("p (b s) -> p b s", b=4)
        MV = small[:, 228:236].rearrange("p (b s) -> p b s", b=4)
        RL = small[:, 236:240]
        EP = small[:, 240:241]
        PIH = small[:, 241:242]
        RT = small[:, 242:246]
        VR = at("vec_rows", [96, P], r_brl)
        LBT = at("lb_work", [P, 64], r_brl + 1 * KB)
        POSI = at("pos_int", [P, T], r_brh, i32)
        ANG = at("angle", [P, T], r_brh + 2 * KB)
        TRN = at("turns", [P, T], r_brh + 4 * KB)
        SH = at("sin_half", [P, T], r_brh + 6 * KB)
        CH = at("cos_half", [P, T], r_brh + 8 * KB)
        OUT = at("out_tokens", [P, TB, D], r_hh)
        FGB = at("final_g_rows", [P, D], r_hh + 16 * KB)

        ID = CST[:, 0:P]
        o_sel = P + 64 * LEVELS
        SEL = CST[0:2, o_sel:o_sel + P]
        FREQ, SIGN2 = (CST[:, o_sel + P + c:o_sel + P + c + 1] for c in (0, 1))

        def mask(lev):
            return CST[:, P + 64 * lev:P + 64 * (lev + 1)].bitcast(i32)

        ng = VC48[:, 0:8]
        bm = VC48[:, 8:32]
        hng, lb, oml, noml = (VC48[:, c:c + 4] for c in (32, 36, 40, 44))

        PJ = [ctx.enter_context(nc.psum_tensor(f"pj{b}", [P, T], f32)) for b in range(NJP)]
        M = [ctx.enter_context(nc.psum_tensor(f"mx{b}", [P, T], f32)) for b in range(5)]

        def sem(name):
            return ctx.enter_context(nc.semaphore(name))

        layer_sems = []

        def lsem(name):
            layer_sems.append(sem(name))
            return layer_sems[-1]

        layer_done = lsem("layer_done")
        raw_in = [lsem(f"raw_in{b}") for b in range(RB)]
        side_in = lsem("side_in")
        w_hi, w_lo, w_lo_vec = lsem("w_hi"), lsem("w_lo"), lsem("w_lo_vec")
        pj_done = lsem("pj_done")
        act_evac, vec_evac = lsem("act_evac"), lsem("vec_evac")
        norm_sum, rstd_ready = lsem("norm_sum"), lsem("rstd_ready")
        full_ready, h_hi = lsem("full_ready"), lsem("h_hi")
        h_lo_pool, h_lo_vec = lsem("h_lo_pool"), lsem("h_lo_vec")
        vec_step, act_step, pool_step = lsem("vec_step"), lsem("act_step"), lsem("pool_step")
        vecs_ready = lsem("vecs_ready")
        rope_done = lsem("rope_done")
        scores_done, negmax_ready, exp_done = lsem("scores_done"), lsem("negmax_ready"), lsem("exp_done")
        probs_ready, pT_done, pT_evac, pv_done = lsem("probs_ready"), lsem("pT_done"), lsem("pT_evac"), lsem("pv_done")
        oa_evac, first_zero = lsem("oa_evac"), lsem("first_zero")
        sig_ready, logf_ready = lsem("sig_ready"), lsem("logf_ready")
        c_keys = lsem("c_keys")
        diff_done, decay_ready, ops_ready = lsem("diff_done"), lsem("decay_ready"), lsem("ops_ready")
        lev_done, at_evac = lsem("lev_done"), lsem("at_evac")
        khat_ready, khT_done, khT_evac = lsem("khat_ready"), lsem("khT_done"), lsem("khT_evac")
        upd_done, state_ready, oc_done = lsem("upd_done"), lsem("state_ready"), lsem("oc_done")
        oc_evac, ocn_done, oc_rstd, oc_ready = lsem("oc_evac"), lsem("ocn_done"), lsem("oc_rstd"), lsem("oc_ready")
        wT_done, wT_evac, wT_ready = lsem("wT_done"), lsem("wT_evac"), lsem("wT_ready")
        ln_stats, ln_rstd, ln_scaled, gv_ready = lsem("ln_stats"), lsem("ln_rstd"), lsem("ln_scaled"), lsem("gv_ready")
        sv_done = lsem("sv_done")
        gated, br_hi, br_lo = lsem("gated"), lsem("br_hi"), lsem("br_lo")
        y_full, y_hi, y_lo = lsem("y_full"), lsem("y_hi"), lsem("y_lo")
        sq_ready, ss_added = lsem("sq_ready"), lsem("ss_added")
        first_num, last_num = layer_sems[0].num, layer_sems[-1].num
        assert last_num - first_num + 1 == len(layer_sems)
        layer_go, layer_seen = sem("layer_go"), sem("layer_seen")
        first_in = [sem(f"first_in{u}") for u in range(RB)]
        first_hi, first_lo, first_lo_vec = sem("first_hi"), sem("first_lo"), sem("first_lo_vec")
        x_in = [sem(f"x_in{tb}") for tb in range(TB)]
        vec_in, cst_in, pos_in = sem("vec_in"), sem("cst_in"), sem("pos_in")
        fill_done, xT_done, xT_evac = sem("fill_done"), sem("xT_done"), sem("xT_evac")
        pro_step = sem("pro_step")
        p_half = sem("p_half")
        p_vec, p_act, p_sq, p_ss = sem("p_vec"), sem("p_act"), sem("p_sq"), sem("p_ss")
        vecT_done, p_diff, p_exp, p_trig, p_sin = sem("vecT_done"), sem("p_diff"), sem("p_exp"), sem("p_trig"), sem("p_sin")
        xT_evac_vec, fg_in = sem("xT_evac_vec"), sem("fg_in")
        e_sum, e_rstd, e_tr, e_evac, out_sent = (sem(n) for n in ("e_sum", "e_rstd", "e_tr", "e_evac", "out_sent"))

        def full(k):
            return (TT if k % 4 < 2 else TP)[:, k % 2, :]

        def evacuated(eng, n):
            which, value = EVAC_NO[n]
            eng.wait_ge(act_evac if which == "a" else vec_evac, value)

        def unit_loads(layer, u):
            kind, i = UNITS[u]

            def w(col, n):
                return w_in[layer, :, col:col + n].rearrange("(k p) c -> p k c", p=P)

            buf = RAW[:, u % RB, :].rearrange("p (k c) -> p k c", c=UC)
            if kind in ("q", "ag"):
                c0 = (AQ if kind == "q" else AG) + 2 * HD * i
                tiles = buf.rearrange("p k (j g d) -> p k g j d", j=2, g=2)
                return [(tiles[:, :, g, j, :], w(c0 + 4 * HD * g + HD * j, HD)) for g in range(2) for j in range(2)]
            if kind == "mix":
                p, n = divmod(i, 3)
                rows = w_branch[layer, n, :, p * UC:(p + 1) * UC]
                if n == 0:
                    r = rows.rearrange("(g j d) c -> g d j c", g=2, j=4)
                    return [(buf[g * HD:(g + 1) * HD, 0:4, :], r[g]) for g in range(2)]
                return [(buf[:, 0:4, :], rows.rearrange("(k p) c -> p k c", p=P))]
            if kind == "out":
                return [(buf, w_out[layer, :, i * UC:(i + 1) * UC].rearrange("(k p) c -> p k c", p=P))]
            if kind in ("k", "v"):
                return [(buf[:, :, 0:P], w(AK if kind == "k" else AV, P))]
            if kind == "merge":
                p, n = divmod(i, 3)
                return [(buf, w(MG + n * D + p * UC, UC))]
            c0 = {"cf": CF, "cq": CQ, "ci": CI, "bv": BV, "bu": BU, "bg": BG, "cg": CG}[kind]
            return [(buf, w(c0 + i * UC, UC))]

        def part(buf, u, half):
            kind = UNITS[u][0]
            kn, cn = (4 if kind == "mix" else KT), (P if kind in ("k", "v") else UC)
            return buf.rearrange("p (k c) -> p k c", c=UC)[:, half * kn // 2:(half + 1) * kn // 2, 0:cn]

        LOADS = [4 if kind in ("q", "ag") else 2 if kind == "mix" and i % 3 == 0 else 1 for kind, i in UNITS]

        def loaded(u):
            return 16 * sum(LOADS[v] for v in range(RB, u + 1) if v % RB == u % RB)

        block = ctx.enter_context(nc.Block())

        @block.sync
        def _(sp):
            sp.dma_start(CST[:, :], consts).then_inc(cst_in, 16)
            sp.dma_start(POSI[:, :], positions[0].partition_broadcast(P)).then_inc(pos_in, 16)
            for tb in range(TB):
                sp.dma_start(XTOK[:, tb, :], x[0, tb * P:(tb + 1) * P, :]).then_inc(x_in[tb], 16)
            for layer in range(DEPTH):
                r0 = 36 * layer
                sp.dma_start(VR[r0:r0 + 8, :], norm_g[layer].rearrange("(k p) -> k p", p=P)).then_inc(vec_in, 16)
                sp.dma_start(VR[r0 + 8:r0 + 32, :],
                             b_merge[layer].rearrange("n (k p) -> (n k) p", p=P)).then_inc(vec_in, 16)
                sp.dma_start(VR[r0 + 32:r0 + 36, :],
                             hgrn_norm_g[layer].rearrange("(k p) -> k p", p=P)).then_inc(vec_in, 16)
            sp.dma_start(VR[72:80, :], hgrn_lb.rearrange("l (k p) -> (l k) p", p=P)).then_inc(vec_in, 16)

            def load_first(layer):
                for u in range(RB):
                    for dst, src in unit_loads(layer, u):
                        sp.dma_start(dst, src).then_inc(first_in[u], 16)

            load_first(0)
            sp.wait_ge(p_trig, 1)
            with sp.Fori(0, DEPTH) as layer:
                sp.dma_start(SPW[:, :, :], sp_w[layer].rearrange("g t s -> t g s")).then_inc(side_in, 16)
                sp.dma_start(LNG[:, :], sp_ln_g[layer].partition_broadcast(P)).then_inc(side_in, 16)
                sp.dma_start(LNB[:, :], sp_ln_b[layer].partition_broadcast(P)).then_inc(side_in, 16)
                sp.dma_start(SPB[:, :, :], sp_b[layer].rearrange("(c g) t -> g c t", g=2)).then_inc(side_in, 16)
                sp.dma_start(SK, attn_sinks[layer].partition_broadcast(P)).then_inc(side_in, 16)
                for u in range(RB, NU):
                    sp.wait_ge(pj_done, JOBS_TO[u - RB])
                    for dst, src in unit_loads(layer, u):
                        sp.dma_start(dst, src).then_inc(raw_in[u % RB], 16)
                for u in range(RB):
                    sp.wait_ge(pj_done, JOBS_TO[NU - RB + u])
                    for dst, src in unit_loads(DEPTH - 1, u):
                        sp.dma_start(dst, src).then_inc(first_in[u], 16)
                sp.drain().then_inc(layer_done, 1)
                sp.wait_ge(layer_go, layer + 1)
                sp.sem_inc(layer_seen, 1)
            sp.dma_start(FGB[:, :], final_g.partition_broadcast(P)).then_inc(fg_in, 16)
            for n in range(2 * TB):
                tb, half = divmod(n, 2)
                c = slice(half * T, (half + 1) * T)
                sp.wait_ge(e_evac, n + 1)
                sp.dma_start(out[0, tb * P:(tb + 1) * P, c], OUT[:, tb, c]).then_inc(out_sent, 16)
            sp.wait_ge(out_sent, 16 * 2 * TB)

        @block.tensor
        def _(pe):
            banks = M + PJ
            pe.wait_ge(cst_in, 16)
            for tb in range(TB):
                pe.wait_ge(x_in[tb], 16)
                for k in range(KT):
                    last = pe.transpose(banks[k][:, tb * P:(tb + 1) * P], XTOK[:, tb, k * P:(k + 1) * P], ID)
                    if tb == TB - 1:
                        last.then_inc(xT_done, 1)
            pe.wait_ge(vec_in, 16 * 7)
            pe.wait_ge(xT_evac, 4)
            pe.wait_ge(xT_evac_vec, 4)
            pe.transpose(M[3][:, 0:80], VR[0:80, :], CST[0:80, 0:80]).then_inc(vecT_done, 1)
            pe.wait_ge(fill_done, 1)
            pe.wait_ge(p_ss, KT)

            def operands(n):
                u, t = JOBS[n]
                kind, i = UNITS[u]
                wh = WHI[:, u % WB, :].rearrange("p (k c) -> p k c", c=UC)
                wl = WLO[:, u % RB, :].rearrange("p (k c) -> p k c", c=UC)
                if kind == "mix":
                    return PJ[n % NJP], wh, wl, BRH[:, i % 3], BRL[:, i % 3], 4
                if kind == "out":
                    return PJ[n % NJP], wh, wl, YH, YL, KT
                return PJ[n % NJP], wh, wl, HH, HL, KT

            def claim(n, layer):
                u, t = JOBS[n]
                if t == 0 and u == 0:
                    pe.wait_ge(first_lo, layer + 1)
                    pe.wait_ge(first_lo_vec, layer + 1)
                elif t == 0:
                    pe.wait_ge(w_lo, u)
                    pe.wait_ge(w_lo_vec, u)
                if n >= NJP:
                    evacuated(pe, n - NJP)

            def three(bank, wh, wl, ah, al, first, final):
                pe.matmul(bank, wh, ah, start=first, stop=False)
                pe.matmul(bank, wh, al, start=False, stop=False)
                return pe.matmul(bank, wl, ah, start=False, stop=final)

            def project_both(n, layer):
                claim(n, layer)
                claim(n + 1, layer)
                for k in range(KT):
                    if n == 0:
                        pe.wait_ge(h_lo_pool if k % 2 else h_lo_vec, k // 2 + 1)
                    else:
                        pe.wait_ge(y_lo, k + 1)
                    for t in range(2):
                        bank, wh, wl, ah, al, kn = operands(n + t)
                        c = slice(t * P, (t + 1) * P)
                        last = three(bank[:, :], wh[:, k, c], wl[:, k, c], ah[:, k, :], al[:, k, :],
                                     k == 0, k == KT - 1)
                        if k == KT - 1:
                            last.then_inc(pj_done, 1)

            def project(n, layer):
                claim(n, layer)
                u, t = JOBS[n]
                kind, i = UNITS[u]
                bank, wh, wl, ah, al, kn = operands(n)
                if kind in ("ci", "bv", "v"):
                    cn, per = (P, 4) if kind == "v" else (UC, 2)
                    for b in range(per):
                        tok = slice((per * t + b) * P, (per * t + b + 1) * P)
                        for k in range(KT):
                            last = three(bank[:, b * cn:(b + 1) * cn], ah[:, k, tok], al[:, k, tok],
                                         wh[:, k, 0:cn], wl[:, k, 0:cn], k == 0, k == KT - 1)
                    last.then_inc(pj_done, 1)
                    return
                if kind == "mix" and i < 3 and t == 0:
                    pe.wait_ge(br_lo, 4 * (i + 1))
                c = slice(t * P, (t + 1) * P)
                for k in range(kn):
                    last = three(bank[:, :], wh[:, k, c], wl[:, k, c], ah[:, k, :], al[:, k, :],
                                 k == 0, k == kn - 1)
                last.then_inc(pj_done, 1)

            def scores(i):
                j, g = divmod(i, 2)
                if i == 0:
                    pe.wait_ge(rope_done, 5)
                else:
                    pe.wait_ge(exp_done, i)
                d = slice(g * HD, (g + 1) * HD)
                for tb in range(TB):
                    q0 = tb * P
                    pe.matmul(M[0][64:128, q0:q0 + P], QP[d, j, q0 + 64:q0 + P], KP[d, q0:q0 + P],
                              start=True, stop=True)
                    last = pe.matmul(M[0][0:64, q0:q0 + 64], QP[d, j, q0:q0 + 64], KP[d, q0:q0 + 64],
                                     start=True, stop=True)
                    if tb > 0:
                        last = pe.matmul(M[0][0:64, q0 + 64:q0 + P], QP[d, j, q0:q0 + 64], KP[d, q0 - 64:q0],
                                         start=True, stop=True)
                last.then_inc(scores_done, 1)

            def transpose_probs(i):
                pe.wait_ge(probs_ready, i + 1)
                if i >= 1:
                    pe.wait_ge(pT_evac, i)
                for tb in range(TB):
                    last = pe.transpose(M[1][:, tb * P:(tb + 1) * P], PR[:, i % 2, tb, :], ID)
                last.then_inc(pT_done, 1)

            def attend(i):
                j, g = divmod(i, 2)
                pe.wait_ge(pT_evac, i + 1)
                pe.wait_ge(first_zero, 1)
                evacuated(pe, FIRST[("v", 0)])
                if g == 0 and j >= 1:
                    pe.wait_ge(oa_evac, j)
                v = slice(g * HD, (g + 1) * HD)
                for tb in range(TB):
                    q0 = tb * P
                    pe.matmul(M[2][g * HD:(g + 1) * HD, q0:q0 + 64], VB[:, tb, v],
                              PT[:, i % 2, q0:q0 + 64], start=True, stop=True)
                    last = pe.matmul(M[2][g * HD:(g + 1) * HD, q0 + 64:q0 + P], VA[:, tb, v],
                                     PT[:, i % 2, q0 + 64:q0 + P], start=True, stop=True)
                last.then_inc(pv_done, 1)

            def diagonal(p):
                evacuated(pe, FIRST[("cq", p)] + 1)
                pe.wait_ge(c_keys, p + 1)
                if p == 1:
                    pe.wait_ge(oc_rstd, 1)
                for hh in range(2):
                    for tb in range(TB):
                        b = slice(tb * P, (tb + 1) * P)
                        last = pe.matmul(M[3 + hh][:, b], KK[p][:, hh, b], QC[p][:, hh, b], start=True, stop=True)
                last.then_inc(lev_done, 1)

            def level(p, lev):
                s = 64 >> lev
                pe.wait_ge(ops_ready, LEVELS * p + lev + 1)
                pe.wait_ge(at_evac, (LEVELS + 1) * p + max(lev, 1))
                ops = XL[lev % 2]
                for hb in range(2 * TB):
                    blk = ops[:, hb * P:(hb + 1) * P]
                    upper = blk.rearrange("p (b u s) -> p b u s", u=2, s=s)[:, :, 1, :]
                    last = pe.matmul(M[3 + lev % 2][:, hb * 64:(hb + 1) * 64], blk, upper, start=True, stop=True)
                last.then_inc(lev_done, 1)

            def transpose_khat(p):
                pe.wait_ge(khat_ready, p + 1)
                pe.wait_ge(at_evac, (LEVELS + 1) * (p + 1))
                for hh in range(2):
                    for c in range(3):
                        last = pe.transpose(M[3 + hh][:, c * P:(c + 1) * P], KK[p][:, hh, c * P:(c + 1) * P], ID)
                last.then_inc(khT_done, 1)

            def state_updates(p):
                pe.wait_ge(khT_evac, p + 1)
                evacuated(pe, FIRST[("ci", p)] + 1)
                for hh in range(2):
                    h = 2 * p + hh
                    for c in range(3):
                        last = pe.matmul(M[3 + hh][:, c * P:(c + 1) * P], KHT[:, hh, c, :],
                                         VC[:, c, h * P:(h + 1) * P], start=True, stop=True)
                last.then_inc(upd_done, 1)

            def recurrent_out(p):
                pe.wait_ge(state_ready, p + 1)
                for hh in range(2):
                    h = 2 * p + hh
                    for tb in range(TB):
                        b = slice(tb * P, (tb + 1) * P)
                        last = pe.matmul(M[3 + hh][:, b], VC[:, tb, h * P:(h + 1) * P], AT[:, hh, b],
                                         start=True, stop=(tb == 0))
                        if tb > 0:
                            last = pe.matmul(M[3 + hh][:, b], ST[:, hh, tb - 1, :], QC[p][:, hh, b],
                                             start=False, stop=True)
                last.then_inc(oc_done, 1)

            def head_norm(p):
                pe.wait_ge(oc_evac, p + 1)
                for hh in range(2):
                    last = pe.matmul(M[3 + hh][:, :], ONE[:, :], AT[:, hh, :], start=True, stop=True)
                last.then_inc(ocn_done, 1)

            def transpose_spatial():
                pe.wait_ge(side_in, 16 * 5)
                pe.wait_ge(pT_evac, A_HEADS)
                for g in range(8):
                    last = pe.transpose(M[g // 4][:, (g % 4) * P:(g % 4 + 1) * P], SPW[:, g, :], ID)
                last.then_inc(wT_done, 1)

            def spatial(ct):
                if ct == 0:
                    pe.wait_ge(wT_ready, 1)
                    pe.wait_ge(gv_ready, 1)
                    pe.wait_ge(oa_evac, 4)
                if ct == 3:
                    pe.wait_ge(gated, SG_JOBS.index(FIRST[("bu", 0)]) + 1)
                bank = M[ct % 3]
                pe.matmul(bank[:, :].rearrange("p (n t) -> p n t", t=P), SEL,
                          SPB[0:2, ct, :].unsqueeze(1).to_broadcast([2, TB, P]), start=True, stop=False,
                          skip_group_check=True)
                for g in range(2):
                    for nb in range(TB):
                        c = (2 * ct + g) * HD
                        last = pe.matmul(bank[g * HD:(g + 1) * HD, nb * P:(nb + 1) * P], GV[:, nb, c:c + HD],
                                         WT[:, 2 * ct + g, :], start=False, stop=(g == 1 and nb == TB - 1),
                                         skip_group_check=True)
                last.then_inc(sv_done, 1)

            hooks = {n: [] for n in range(NJ)}
            for i in range(A_HEADS):
                hooks[10 + i].append((attend, i))
            for i in range(A_HEADS):
                hooks[9 + i].append((transpose_probs, i))
            for i in range(A_HEADS):
                hooks[7 + i].append((scores, i))
            for p, d in enumerate(DIAG):
                hooks[d].append((diagonal, p))
                for lev in range(LEVELS):
                    hooks[d + 1 + lev].append((level, p, lev))
                for step, f in enumerate((transpose_khat, state_updates, recurrent_out, head_norm)):
                    hooks[d + 1 + LEVELS + step].append((f, p))
            hooks[18].append((transpose_spatial,))
            for ct in range(4):
                hooks[25 + ct].append((spatial, ct))

            with pe.Fori(0, DEPTH) as layer:
                pe.matmul(M[4][:, :], ONE[:, :], SS[:, :], start=True, stop=True).then_inc(norm_sum, 1)
                for n in range(NJ):
                    if n in (0, FIRST[("out", 0)]):
                        project_both(n, layer)
                    elif n not in (1, FIRST[("out", 0)] + 1):
                        project(n, layer)
                    for f, *a in hooks[n]:
                        f(*a)
                pe.drain().then_inc(layer_done, 1)
                pe.wait_ge(layer_go, layer + 1)

            for tb in range(TB):
                last = pe.matmul(M[4][:, tb:tb + 1], SS[:, tb * P:(tb + 1) * P], ONE[:, 0:1], start=True, stop=True)
            last.then_inc(e_sum, 1)
            banks = PJ + M[0:4]
            for n in range(2 * TB):
                tb, half = divmod(n, 2)
                if n >= len(banks):
                    pe.wait_ge(e_evac, n - len(banks) + 1)
                for c in range(4):
                    last = pe.transpose(banks[n % len(banks)][:, c * P:(c + 1) * P],
                                        XT[:, 4 * half + c, tb * P:(tb + 1) * P], ID)
                last.then_inc(e_tr, 1)

        @block.scalar
        def _(act):
            steps = [0]

            def chained(ins):
                steps[0] += 1
                ins.then_inc(act_step, 1)
                act.wait_ge(act_step, steps[0])

            act.wait_ge(fill_done, 1)
            act.wait_ge(p_half, 1)
            act.activation(SH[:, :], ANG[:, :], ACT.Sin)
            act.activation(CH[:, :], TRN[:, :], ACT.Sin, bias=PIH, scale=-1.0).then_inc(p_sin, 1)
            banks = M + PJ
            for k in range(0, KT, 2):
                act.wait_ge(xT_done, k + 1)
                act.activation(XT[:, k, :], banks[k][:, :], ACT.Copy).then_inc(xT_evac, 1)
            for k in range(KT):
                if k % 2:
                    act.wait_ge(xT_evac_vec, k // 2 + 1)
                else:
                    act.wait_ge(xT_evac, k // 2 + 1)
                if k >= 2:
                    act.wait_ge(p_ss, k - 1)
                act.activation(TP[:, k % 2, :], XT[:, k, :], ACT.Square).then_inc(p_sq, 1)

            def split_first(value):
                act.wait_ge(first_in[0], value)
                for half in range(2):
                    act.activation(part(WHI[:, 0, :], 0, half), part(RAW[:, 0, :], 0, half), ACT.Copy)\
                       .then_inc(first_hi, 1)

            split_first(16 * LOADS[0])
            act.wait_ge(p_diff, 1)
            act.activation(LBT[:, 12:20], LBT[:, 4:12], ACT.Exp).then_inc(p_exp, 1)

            def rsqrt(dst, src, scale):
                chained(act.activation(dst, src, ACT.Ln, bias=EP, scale=scale))
                return act.activation(dst, dst, ACT.Exp, scale=-0.5)

            def split_hi(u, layer):
                if u < RB:
                    act.wait_ge(first_in[u], 16 * LOADS[u] * (layer + 1))
                else:
                    act.wait_ge(raw_in[u % RB], loaded(u))
                if u >= WB:
                    act.wait_ge(pj_done, JOBS_TO[u - WB])
                for half in range(2):
                    act.activation(part(WHI[:, u % WB, :], u, half), part(RAW[:, u % RB, :], u, half), ACT.Copy)\
                       .then_inc(w_hi, 1)

            def evac(n):
                u, t = JOBS[n]
                kind, i = UNITS[u]
                src = PJ[n % NJP][:, :]
                done = act_evac
                if kind in BY_VECTOR:
                    return
                act.wait_ge(pj_done, n + 1)
                if kind in ("q", "k"):
                    if n >= 2:
                        act.wait_ge(rope_done, n - 1)
                    for a in range(0, P, HD):
                        b, c = a + HD // 2, a + HD
                        act.activation(QS[a:b, n % 2, :], src[b:c], ACT.Copy)
                        act.activation(QS[b:c, n % 2, :], src[a:b], ACT.Copy)
                    act.activation(QR[:, n % 2, :], src, ACT.Copy).then_inc(done, 1)
                elif kind == "v":
                    v = src.rearrange("p (b c) -> p b c", b=TB)
                    act.activation(VB[0:64, :, :], v[0:64], ACT.Copy)
                    act.activation(VB[64:128, 1:TB, :], v[64:128, 0:TB - 1], ACT.Copy)
                    act.activation(VA[:, :, :], v, ACT.Copy).then_inc(done, 1)
                elif kind == "cq":
                    act.activation(QC[i][:, t, :], src, ACT.Copy).then_inc(done, 1)
                elif kind == "ci":
                    act.activation(VC[:, 2 * t:2 * t + 2, i * UC:(i + 1) * UC],
                                   src.rearrange("p (b c) -> p b c", b=2), ACT.Copy).then_inc(done, 1)
                elif kind == "bv":
                    if i == 0 and t == 0:
                        act.wait_ge(scores_done, A_HEADS)
                    act.activation(GV[:, 2 * t:2 * t + 2, i * UC:(i + 1) * UC],
                                   src.rearrange("p (b c) -> p b c", b=2), ACT.Gelu_apprx_tanh).then_inc(done, 1)
                elif kind in ("ag", "bg", "cg", "bu"):
                    s = SG_JOBS.index(n)
                    if s >= 2:
                        act.wait_ge(gated, s - 1)
                    fn = ACT.Gelu_apprx_tanh if kind == "bu" else ACT.Silu
                    act.activation(SG[:, s % 2, :], src, fn).then_inc(done, 1)
                else:
                    p, b = divmod(i, 3)
                    if i >= 2:
                        evacuated(act, FIRST[("mix", i - 2)] + 1)
                    c = 8 * b + 2 * p + t
                    act.activation(GM[:, i % 2, t, :], src, ACT.Sigmoid, bias=bm[:, c:c + 1]).then_inc(done, 1)

            def softmax_exp(i):
                head = i // 2 + 4 * (i % 2)
                act.wait_ge(negmax_ready, i + 1)
                if i >= 2:
                    act.wait_ge(pT_done, i - 1)
                for tb in range(TB):
                    act.activation(PR[:, i % 2, tb, :], M[0][:, tb * P:(tb + 1) * P], ACT.Exp,
                                   bias=NM[:, i % 2, tb:tb + 1], scale=SCALE, accum_out=SM[:, i % 2, tb:tb + 1])
                act.activation(ES[:, i % 2, :], NM[:, i % 2, :], ACT.Exp, bias=SK[:, head:head + 1])\
                   .then_inc(exp_done, 1)

            def probsT_out(i):
                act.wait_ge(pT_done, i + 1)
                if i >= 2:
                    act.wait_ge(pv_done, i - 1)
                act.activation(PT[:, i % 2, :], M[1][:, :], ACT.Copy).then_inc(pT_evac, 1)

            def forget(p):
                evacuated(act, FIRST[("cf", p)] + 1)
                act.activation(KK[p][:, :, :], BC[p][:, :, :], ACT.Sigmoid).then_inc(sig_ready, 1)
                act.wait_ge(sig_ready, p + 1)
                for hh in range(2):
                    h = 2 * p + hh
                    last = act.activation(BC[p][:, hh, :], KK[p][:, hh, :], ACT.Ln,
                                          bias=lb[:, h:h + 1], scale=oml[:, h:h + 1])
                last.then_inc(logf_ready, 1)

            def decay_exp(p, lev):
                act.wait_ge(diff_done, (LEVELS + 1) * p + lev + 1)
                act.activation(E[lev % 2][:, :], E[lev % 2][:, :], ACT.Exp).then_inc(decay_ready, 1)

            def block_exp(p):
                act.wait_ge(diff_done, (LEVELS + 1) * (p + 1))
                act.wait_ge(ops_ready, LEVELS * (p + 1))
                act.activation(E[1][:, 0:6 * P], E[1][:, 0:6 * P], ACT.Exp)
                act.activation(E[0][:, :], BC[p][:, :, :].rearrange("p h t -> p (h t)"), ACT.Exp)\
                   .then_inc(decay_ready, 1)

            def khatT_out(p):
                act.wait_ge(khT_done, p + 1)
                if p == 1:
                    act.wait_ge(upd_done, 1)
                for hh in range(2):
                    last = act.activation(KHT[:, hh, :, :], M[3 + hh][:, 0:3 * P].rearrange("p (c d) -> p c d", c=3),
                                          ACT.Copy)
                last.then_inc(khT_evac, 1)

            def recurrent_evac(p):
                act.wait_ge(oc_done, p + 1)
                for hh in range(2):
                    act.activation(OX[:, 2, 2 * p + hh, :], M[3 + hh][:, :], ACT.Copy)
                    last = act.activation(AT[:, hh, :], M[3 + hh][:, :], ACT.Square)
                last.then_inc(oc_evac, 1)

            def head_rstd(p):
                act.wait_ge(ocn_done, p + 1)
                for hh in range(2):
                    last = act.activation(AT[:, hh, :], M[3 + hh][:, :], ACT.Ln, bias=EP, scale=1.0 / P)
                chained(last)
                act.activation(AT[:, :, :], AT[:, :, :], ACT.Exp, scale=-0.5).then_inc(oc_rstd, 1)

            def spatialT_out():
                act.wait_ge(wT_done, 1)
                act.wait_ge(pv_done, A_HEADS)
                for b in range(2):
                    last = act.activation(WT[:, 4 * b:4 * b + 4, :],
                                          M[b][:, :].rearrange("p (g t) -> p g t", g=4), ACT.Copy)
                last.then_inc(wT_evac, 1)

            def ln_rsqrt():
                act.wait_ge(ln_stats, 1)
                rsqrt(RL, MV[:, :, 1], 1.0).then_inc(ln_rstd, 1)

            def branch_hi(n):
                gi = GATE_JOBS.index(n)
                act.wait_ge(gated, SG_JOBS.index(n) + 1)
                kind = KIND[n]
                ct = n - FIRST[(kind, 0)]
                act.activation(BRH[:, BRANCH[kind], ct, :], TT[:, gi % 2, :], ACT.Copy).then_inc(br_hi, 1)

            def y_high(m):
                act.wait_ge(y_full, m + 1)
                act.activation(YH[:, m, :], TT[:, m % 2, :], ACT.Copy).then_inc(y_hi, 1)

            def square_x(m):
                evacuated(act, FIRST[("out", 0)] + m)
                if m >= 2:
                    act.wait_ge(ss_added, m - 1)
                act.activation(TP[:, m % 2, :], XT[:, m, :], ACT.Square).then_inc(sq_ready, 1)

            phase = {n: [] for n in range(NJ + 4)}
            for i in range(A_HEADS):
                phase[10 + i].append((probsT_out, i))
                phase[8 + i].append((softmax_exp, i))
            for p, d in enumerate(DIAG):
                phase[FIRST[("cf", p)] + 2].append((forget, p))
                for lev in range(LEVELS):
                    phase[d - 1 + lev].append((decay_exp, p, lev))
                phase[d + LEVELS].append((block_exp, p))
                phase[d + LEVELS + 2].append((khatT_out, p))
                phase[d + LEVELS + 4].append((recurrent_evac, p))
                phase[d + LEVELS + 5].append((head_rstd, p))
            phase[19].append((spatialT_out,))
            phase[22].append((ln_rsqrt,))
            for n in GATE_JOBS:
                phase[n + 1].append((branch_hi, n))
            for m in range(KT):
                phase[FIRST[("mix", 3 * (m // 2) + 2)] + 1 + m % 2].append((y_high, m))
                phase[FIRST[("out", 0)] + m + 1].append((square_x, m))

            with act.Fori(0, DEPTH) as layer:
                steps[0] = 0
                act.wait_ge(norm_sum, 1)
                rsqrt(RS[:, :], M[4][:, :], 1.0 / D).then_inc(rstd_ready, 1)
                for k in range(KT):
                    act.wait_ge(full_ready, k + 1)
                    act.activation(HH[:, k, :], full(k), ACT.Copy).then_inc(h_hi, 1)
                split_hi(1, layer)
                act.wait_ge(side_in, 16 * 5)
                for n in range(NJ + 4):
                    if n < NJ and n > 0 and JOBS[n][1] == 0 and JOBS[n][0] + 1 < NU:
                        split_hi(JOBS[n][0] + 1, layer)
                    for f, *a in phase[n]:
                        f(*a)
                    if n < NJ:
                        evac(n)
                    if n == JOBS_TO[NU - 2]:
                        split_first(16 * LOADS[0] * (layer + 2))
                act.drain().then_inc(layer_done, 1)
                act.wait_ge(layer_go, layer + 1)

            act.wait_ge(e_sum, 1)
            act.activation(RT, M[4][:, 0:TB], ACT.Ln, bias=EP, scale=1.0 / D).then_inc(p_act, 1)
            act.wait_ge(p_act, 1)
            act.activation(RT, RT, ACT.Exp, scale=-0.5).then_inc(e_rstd, 1)

        @block.gpsimd
        def _(pool):
            pool.memset(ONE[:, :], 1.0)
            pool.memset(EP, EPS)
            pool.memset(PIH, float(np.pi / 2)).then_inc(fill_done, 1)

            def sub(dst, full, hi):
                return pool.tensor_tensor(out=dst, in0=full, in1=hi.bitcast(f32), op=ALU.subtract)

            def split_lo(u):
                pool.wait_ge(w_hi, 2 * u - 1)
                sub(part(WLO[:, u % RB, :], u, 0), part(RAW[:, u % RB, :], u, 0), part(WHI[:, u % WB, :], u, 0))\
                    .then_inc(w_lo, 1)

            def split_first(value):
                pool.wait_ge(first_hi, value)
                sub(part(WLO[:, 0, :], 0, 0), part(RAW[:, 0, :], 0, 0), part(WHI[:, 0, :], 0, 0))\
                    .then_inc(first_lo, 1)

            split_first(1)

            def ln_affine():
                pool.wait_ge(side_in, 16 * 5)
                pool.wait_ge(ln_scaled, 1)
                pool.tensor_tensor(out=GV[:, :, :], in0=GV[:, :, :], op=ALU.mult,
                                   in1=LNG[:, :].unsqueeze(1).to_broadcast([P, TB, T])).then_inc(pool_step, 1)
                pool.wait_ge(pool_step, 1)
                pool.tensor_tensor(out=GV[:, :, :], in0=GV[:, :, :], op=ALU.add,
                                   in1=LNB[:, :].unsqueeze(1).to_broadcast([P, TB, T])).then_inc(gv_ready, 1)

            def branch_lo(n):
                gi = GATE_JOBS.index(n)
                pool.wait_ge(br_hi, gi + 1)
                kind = KIND[n]
                ct = n - FIRST[(kind, 0)]
                if kind == "bg" and ct == 0:
                    pool.wait_ge(oc_done, 1)
                if kind == "cg" and ct == 0:
                    pool.wait_ge(oc_done, 2)
                sub(BRL[:, BRANCH[kind], ct, :], TT[:, gi % 2, :], BRH[:, BRANCH[kind], ct, :]).then_inc(br_lo, 1)

            def y_low(m):
                pool.wait_ge(y_hi, m + 1)
                sub(YL[:, m, :], TT[:, m % 2, :], YH[:, m, :]).then_inc(y_lo, 1)

            phase = {n: [] for n in range(NJ + 4)}
            phase[23].append((ln_affine,))
            for n in GATE_JOBS:
                phase[n + 1].append((branch_lo, n))
            for m in range(KT):
                phase[FIRST[("mix", 3 * (m // 2) + 2)] + 1 + m % 2].append((y_low, m))

            with pool.Fori(0, DEPTH) as layer:
                for k in range(1, KT, 2):
                    pool.wait_ge(h_hi, k + 1)
                    sub(HL[:, k, :], full(k), HH[:, k, :]).then_inc(h_lo_pool, 1)
                split_lo(1)
                for n in range(NJ + 4):
                    if n < NJ and n > 0 and JOBS[n][1] == 0 and JOBS[n][0] + 1 < NU:
                        split_lo(JOBS[n][0] + 1)
                    for f, *a in phase[n]:
                        f(*a)
                split_first(2 * layer + 3)
                pool.drain()
                pool.wait_ge(layer_done, 4)
                pool.sem_clear(range(first_num, last_num + 1))
                pool.sem_inc(layer_go, 1)

        @block.vector
        def _(dve):
            steps = [0]

            def chained(ins):
                steps[0] += 1
                ins.then_inc(vec_step, 1)
                dve.wait_ge(vec_step, steps[0])

            psteps = [0]

            def pchain(ins):
                psteps[0] += 1
                ins.then_inc(pro_step, 1)
                dve.wait_ge(pro_step, psteps[0])

            dve.wait_ge(pos_in, 16)
            dve.wait_ge(cst_in, 16)
            pchain(dve.tensor_copy(ANG[:, :], POSI[:, :]))
            pchain(dve.tensor_scalar(ANG[:, :], ANG[:, :], FREQ, None, ALU.mult))
            magic = 1.5 * 2.0 ** 23
            two_pi = 2.0 * np.pi
            c1 = 6.28125
            c2 = float(np.float32(np.round((two_pi - c1) * 2.0 ** 21) / 2.0 ** 21))
            c3 = float(np.float32(two_pi - c1 - c2))
            pchain(dve.tensor_scalar(TRN[:, :], ANG[:, :], float(1.0 / two_pi), magic, ALU.mult, ALU.add))
            pchain(dve.tensor_scalar(TRN[:, :], TRN[:, :], -magic, None, ALU.add))
            for c in (c1, c2, c3):
                pchain(dve.scalar_tensor_tensor(out=ANG[:, :], in0=TRN[:, :], scalar=-c, in1=ANG[:, :],
                                                op0=ALU.mult, op1=ALU.add))
            pchain(dve.tensor_scalar(ANG[:, :], ANG[:, :], 0.5, None, ALU.mult))
            dve.scalar_tensor_tensor(out=TRN[:, :], in0=ANG[:, :], scalar=-1.0, in1=ANG[:, :],
                                     op0=ALU.mult, op1=ALU.max).then_inc(p_half, 1)
            banks = M + PJ
            for k in range(1, KT, 2):
                dve.wait_ge(xT_done, k + 1)
                dve.tensor_copy(XT[:, k, :], banks[k][:, :]).then_inc(xT_evac_vec, 1)
            for k in range(KT):
                dve.wait_ge(p_sq, k + 1)
                if k == 0:
                    dve.tensor_copy(SS[:, :], TP[:, 0, :]).then_inc(p_ss, 1)
                else:
                    dve.wait_ge(p_ss, k)
                    dve.tensor_tensor(out=SS[:, :], in0=SS[:, :], in1=TP[:, k % 2, :], op=ALU.add).then_inc(p_ss, 1)
            def split_first(value):
                dve.wait_ge(first_hi, value)
                dve.tensor_tensor(out=part(WLO[:, 0, :], 0, 1), in0=part(RAW[:, 0, :], 0, 1),
                                  in1=part(WHI[:, 0, :], 0, 1).bitcast(f32), op=ALU.subtract).then_inc(first_lo_vec, 1)

            split_first(2)
            dve.wait_ge(vecT_done, 1)
            dve.tensor_copy(LBT[:, 24:32], M[3][:, 72:80])
            dve.tensor_copy(VL[:, :, 0:36], M[3][:, 0:72].rearrange("p (l c) -> p l c", l=2)).then_inc(p_vec, 1)
            L0, L1, mx = LBT[:, 24:28], LBT[:, 28:32], LBT[:, 0:4]
            dve.wait_ge(p_vec, 1)
            pchain(dve.tensor_tensor(out=mx, in0=L0, in1=L1, op=ALU.max))
            dve.tensor_tensor(out=LBT[:, 4:8], in0=L0, in1=mx, op=ALU.subtract)
            dve.tensor_tensor(out=LBT[:, 8:12], in0=L1, in1=mx, op=ALU.subtract).then_inc(p_diff, 1)
            dve.wait_ge(p_exp, 1)
            e0, e1, sm, p0, p1 = (LBT[:, c:c + 4] for c in (12, 16, 32, 36, 40))
            pchain(dve.tensor_tensor(out=sm, in0=e0, in1=e1, op=ALU.add))
            pchain(dve.reciprocal(sm, sm))
            pchain(dve.tensor_tensor(out=p0, in0=e0, in1=sm, op=ALU.mult))
            pchain(dve.tensor_tensor(out=p1, in0=e1, in1=sm, op=ALU.mult))
            pchain(dve.tensor_tensor(out=p1, in0=p0, in1=p1, op=ALU.add))
            pchain(dve.tensor_tensor(out=VL[:, 0, 36:40], in0=p0, in1=p0, op=ALU.subtract))
            pchain(dve.tensor_tensor(out=VL[:, 1, 36:40], in0=p1, in1=p0, op=ALU.subtract))
            pchain(dve.tensor_scalar(VL[:, :, 36:40], VL[:, :, 36:40], 0.0, 1.0, ALU.max, ALU.min))
            pchain(dve.tensor_scalar(VL[:, :, 40:44], VL[:, :, 36:40], -1.0, 1.0, ALU.mult, ALU.add))
            pchain(dve.tensor_scalar(VL[:, :, 44:48], VL[:, :, 40:44], -1.0, None, ALU.mult))
            dve.wait_ge(p_sin, 1)
            pchain(dve.tensor_tensor(out=SIN[:, :], in0=SH[:, :], in1=CH[:, :], op=ALU.mult))
            pchain(dve.tensor_scalar(SIN[:, :], SIN[:, :], SIGN2, None, ALU.mult))
            pchain(dve.tensor_tensor(out=COS[:, :], in0=SH[:, :], in1=SH[:, :], op=ALU.mult))
            dve.tensor_scalar(COS[:, :], COS[:, :], -2.0, 1.0, ALU.mult, ALU.add).then_inc(p_trig, 1)
            dve.wait_ge(p_trig, 1)
            dve.wait_ge(p_ss, KT)

            def evac(n):
                u, t = JOBS[n]
                kind, i = UNITS[u]
                if kind not in BY_VECTOR:
                    return
                src = PJ[n % NJP][:, :]
                dve.wait_ge(pj_done, n + 1)
                if kind == "cf":
                    dve.tensor_scalar(BC[i][:, t, :], src, -44.0, None, ALU.max).then_inc(vec_evac, 1)
                elif kind == "mix":
                    p, b = divmod(i, 3)
                    evacuated(dve, FIRST[("merge", i)] + t)
                    if b == 0:
                        if p == 0:
                            dve.wait_ge(br_lo, 12)
                            dve.wait_ge(oc_ready, 2)
                        else:
                            dve.wait_ge(y_lo, 2 * p)
                        dve.tensor_tensor(out=TT[:, t, :], in0=src, in1=GM[:, i % 2, t, :], op=ALU.mult)\
                           .then_inc(vec_evac, 1)
                        return
                    dve.tensor_tensor(out=TP[:, t, :], in0=src, in1=GM[:, i % 2, t, :], op=ALU.mult)\
                       .then_inc(vec_evac, 1)
                    evacuated(dve, n)
                    add = dve.tensor_tensor(out=TT[:, t, :], in0=TT[:, t, :], in1=TP[:, t, :], op=ALU.add)
                    if b == 2:
                        add.then_inc(y_full, 1)
                    else:
                        chained(add)
                else:
                    m = 2 * i + t
                    if m == 0:
                        dve.wait_ge(full_ready, KT)
                    dve.tensor_tensor(out=XT[:, m, :], in0=src, in1=XT[:, m, :], op=ALU.add).then_inc(vec_evac, 1)

            def split_lo(u):
                dve.wait_ge(w_hi, 2 * u)
                dve.tensor_tensor(out=part(WLO[:, u % RB, :], u, 1), in0=part(RAW[:, u % RB, :], u, 1),
                                  in1=part(WHI[:, u % WB, :], u, 1).bitcast(f32), op=ALU.subtract).then_inc(w_lo_vec, 1)

            def rope(r):
                evacuated(dve, r)
                if r >= 1:
                    dve.wait_ge(rope_done, r)
                else:
                    dve.wait_ge(h_lo_vec, 4)
                    dve.wait_ge(h_lo_pool, 4)
                dst = QP[:, r, :] if r < 4 else KP[:, :]
                dve.tensor_tensor(out=R1[:, :], in0=QR[:, r % 2, :], in1=COS[:, :], op=ALU.mult)
                chained(dve.tensor_tensor(out=R2[:, :], in0=QS[:, r % 2, :], in1=SIN[:, :], op=ALU.mult))
                dve.tensor_tensor(out=dst, in0=R1[:, :], in1=R2[:, :], op=ALU.add).then_inc(rope_done, 1)

            def neg_max(i):
                head = i // 2 + 4 * (i % 2)
                dve.wait_ge(scores_done, i + 1)
                chained(dve.memset(M[0][0:64, 64:128], MASK_VALUE))
                if i >= 1:
                    dve.wait_ge(negmax_ready, i)
                chained(dve.reduce_max(MX, M[0][:, :].rearrange("p (b k) -> p b k", b=TB), AX))
                if i >= 2:
                    dve.wait_ge(exp_done, i - 1)
                dve.tensor_scalar(NM[:, i % 2, :], MX, -SCALE, NSK[:, head:head + 1], ALU.mult, ALU.min)\
                   .then_inc(negmax_ready, 1)

            def normalise(i):
                dve.wait_ge(exp_done, i + 1)
                if i >= 1:
                    dve.wait_ge(probs_ready, i)
                chained(dve.tensor_tensor(out=DN, in0=SM[:, i % 2, :], in1=ES[:, i % 2, :], op=ALU.add))
                chained(dve.reciprocal(RD, DN))
                dve.tensor_tensor(out=PR[:, i % 2, :, :], in0=PR[:, i % 2, :, :],
                                  in1=RD.unsqueeze(2).to_broadcast([P, TB, P]), op=ALU.mult).then_inc(probs_ready, 1)

            def attn_out(j):
                dve.wait_ge(pv_done, 2 * j + 2)
                dve.tensor_copy(OX[:, 0, j, :], M[2][:, :]).then_inc(oa_evac, 1)

            def keys_and_sums(p):
                dve.wait_ge(logf_ready, p + 1)
                for hh in range(2):
                    h = 2 * p + hh
                    dve.tensor_scalar(KK[p][:, hh, :], KK[p][:, hh, :], noml[:, h:h + 1], oml[:, h:h + 1],
                                      ALU.mult, ALU.add)
                for hh in range(2):
                    for tb in range(TB):
                        b = BC[p][:, hh, tb * P:(tb + 1) * P]
                        last = dve.tensor_tensor_scan(b, ONE[:, :], b, 0.0, ALU.mult, ALU.add)
                last.then_inc(c_keys, 1)
                dve.wait_ge(c_keys, p + 1)

            def halves(a, s):
                return a.rearrange("p (b u s) -> p b u s", u=2, s=s)

            def diffs(p, lev):
                s = 64 >> lev
                b = halves(BC[p][:, :, :].rearrange("p h t -> p (h t)"), s)
                e = halves(E[lev % 2][:, :], s)
                if (p, lev) == (0, 0):
                    dve.wait_ge(rope_done, 5)
                elif lev >= 2:
                    dve.wait_ge(ops_ready, LEVELS * p + lev - 1)
                elif p == 1:
                    dve.wait_ge(state_ready, 1)
                mid = b[:, :, 0, s - 1:s].to_broadcast([P, 1024 // (2 * s), s])
                dve.tensor_tensor(out=e[:, :, 0, :], in0=mid, in1=b[:, :, 0, :], op=ALU.subtract)
                dve.tensor_tensor(out=e[:, :, 1, :], in0=b[:, :, 1, :], in1=mid, op=ALU.subtract).then_inc(diff_done, 1)

            def operands(p, lev):
                s = 64 >> lev
                n = LEVELS * p + lev
                dve.wait_ge(decay_ready, (LEVELS + 1) * p + lev + 1)
                if n >= 2:
                    q, back = divmod(n - 2, LEVELS)
                    dve.wait_ge(lev_done, (LEVELS + 1) * q + back + 2)
                e, o = halves(E[lev % 2][:, :], s), halves(XL[lev % 2][:, :], s)
                k, q = (halves(a[p][:, :, :].rearrange("p h t -> p (h t)"), s) for a in (KK, QC))
                dve.tensor_tensor(out=o[:, :, 0, :], in0=k[:, :, 0, :], in1=e[:, :, 0, :], op=ALU.mult)
                if lev == 0:
                    evacuated(dve, FIRST[("cq", p)] + 1)
                dve.tensor_tensor(out=o[:, :, 1, :], in0=q[:, :, 1, :], in1=e[:, :, 1, :], op=ALU.mult)\
                   .then_inc(ops_ready, 1)

            def take_diagonal(p):
                dve.wait_ge(lev_done, (LEVELS + 1) * p + 1)
                if p == 0:
                    dve.wait_ge(rope_done, 5)
                else:
                    dve.wait_ge(oc_ready, 1)
                for hh in range(2):
                    last = dve.tensor_tensor(out=AT[:, hh, :].rearrange("p (b t) -> p b t", b=TB),
                                             in0=M[3 + hh][:, :].rearrange("p (b t) -> p b t", b=TB),
                                             in1=ID.unsqueeze(1).to_broadcast([P, TB, P]), op=ALU.mult)
                last.then_inc(at_evac, 1)

            def take_level(p, lev):
                s = 64 >> lev
                dve.wait_ge(lev_done, (LEVELS + 1) * p + lev + 2)
                dve.wait_ge(at_evac, (LEVELS + 1) * p + lev + 1)
                dst = AT[:, :, :].rearrange("p h (b u s) -> p (h b) u s", u=2, s=s)[:, :, 1, :]
                nb = 64 // s
                src = M[3 + lev % 2][:, :].rearrange("p (c b s) -> p c b s", b=nb, s=s)
                dst = dst.rearrange("p (c b) s -> p c b s", b=nb)
                msk = mask(lev).rearrange("p (b s) -> p b s", s=s).unsqueeze(1).to_broadcast([P, 2 * TB, nb, s])
                dve.copy_predicated(dst, msk, src).then_inc(at_evac, 1)

            def block_diffs(p):
                b = BC[p][:, :, :].rearrange("p h (c t) -> p h c t", t=P)
                dve.wait_ge(ops_ready, LEVELS * (p + 1) - 1)
                for hh in range(2):
                    last = dve.tensor_tensor(out=E[1][:, hh * 3 * P:(hh + 1) * 3 * P].rearrange("p (c t) -> p c t", t=P),
                                             in0=b[:, hh, 0:3, P - 1:P].to_broadcast([P, 3, P]),
                                             in1=b[:, hh, 0:3, :], op=ALU.subtract)
                last.then_inc(diff_done, 1)

            def decayed(p):
                dve.wait_ge(decay_ready, (LEVELS + 1) * (p + 1))
                dve.wait_ge(lev_done, (LEVELS + 1) * p + 1)
                dve.wait_ge(ops_ready, LEVELS * (p + 1))
                for hh in range(2):
                    dve.tensor_tensor(out=KK[p][:, hh, 0:3 * P], in0=KK[p][:, hh, 0:3 * P],
                                      in1=E[1][:, hh * 3 * P:(hh + 1) * 3 * P], op=ALU.mult)
                dve.tensor_tensor(out=QC[p][:, :, :].rearrange("p h t -> p (h t)"),
                                  in0=QC[p][:, :, :].rearrange("p h t -> p (h t)"), in1=E[0][:, :], op=ALU.mult)\
                   .then_inc(khat_ready, 1)

            def states(p):
                dve.wait_ge(upd_done, p + 1)
                if p == 1:
                    dve.wait_ge(oc_done, 1)
                for hh in range(2):
                    chained(dve.tensor_copy(ST[:, hh, 0, :], M[3 + hh][:, 0:P]))
                for c in (1, 2):
                    for hh in range(2):
                        eb = E[0][:, hh * T + (c + 1) * P - 1:hh * T + (c + 1) * P]
                        last = dve.scalar_tensor_tensor(out=ST[:, hh, c, :], in0=ST[:, hh, c - 1, :], scalar=eb,
                                                        in1=M[3 + hh][:, c * P:(c + 1) * P],
                                                        op0=ALU.mult, op1=ALU.add)
                        if (c, hh) != (2, 1):
                            chained(last)
                last.then_inc(state_ready, 1)

            def head_scaled(p):
                dve.wait_ge(oc_rstd, p + 1)
                for hh in range(2):
                    h = 2 * p + hh
                    last = dve.scalar_tensor_tensor(out=OX[:, 2, h, :], in0=OX[:, 2, h, :], scalar=hng[:, h:h + 1],
                                                    in1=AT[:, hh, :], op0=ALU.mult, op1=ALU.mult)
                last.then_inc(oc_ready, 1)

            def spatial_mask():
                dve.wait_ge(wT_evac, 1)
                dve.memset(WT[64:128, :, 0:64], 0.0).then_inc(wT_ready, 1)

            def layer_norm_stats():
                evacuated(dve, FIRST[("bv", 1)] + 1)
                for tb in range(TB):
                    last = dve.bn_stats(BS[:, tb, :], GV[:, tb, :])
                chained(last)
                for tb in range(TB):
                    last = dve.bn_aggr(MV[:, tb, :], BS[:, tb, :])
                last.then_inc(ln_stats, 1)

            def layer_norm_scale():
                dve.wait_ge(ln_rstd, 1)
                for tb in range(TB):
                    last = dve.tensor_scalar(GV[:, tb, :], GV[:, tb, :], MV[:, tb, 0:1], RL[:, tb:tb + 1],
                                             ALU.subtract, ALU.mult)
                last.then_inc(ln_scaled, 1)

            def gate_product(n):
                s = SG_JOBS.index(n)
                kind = KIND[n]
                ct = n - FIRST[(kind, 0)]
                evacuated(dve, n)
                if kind == "bu":
                    dve.wait_ge(sv_done, ct + 1)
                    dve.tensor_tensor(out=OX[:, 1, ct, :], in0=M[ct % 3][:, :], in1=SG[:, s % 2, :], op=ALU.mult)\
                       .then_inc(gated, 1)
                    return
                gi = GATE_JOBS.index(n)
                if gi >= 2:
                    dve.wait_ge(br_lo, gi - 1)
                br = BRANCH[kind]
                if kind == "ag":
                    dve.wait_ge(oa_evac, ct + 1)
                if kind == "bg":
                    dve.wait_ge(gated, SG_JOBS.index(FIRST[("bu", 0)] + ct) + 1)
                if kind == "cg":
                    dve.wait_ge(oc_ready, ct // 2 + 1)
                dve.tensor_tensor(out=TT[:, gi % 2, :], in0=OX[:, br, ct, :], in1=SG[:, s % 2, :], op=ALU.mult)\
                   .then_inc(gated, 1)

            def sum_squares(m):
                dve.wait_ge(sq_ready, m + 1)
                if m == 0:
                    dve.wait_ge(state_ready, 2)
                    dve.tensor_copy(SS[:, :], TP[:, 0, :]).then_inc(ss_added, 1)
                else:
                    dve.wait_ge(ss_added, m)
                    dve.tensor_tensor(out=SS[:, :], in0=SS[:, :], in1=TP[:, m % 2, :], op=ALU.add).then_inc(ss_added, 1)

            phase = {n: [] for n in range(NJ + 4)}
            for r in range(5):
                phase[r + 1].append((rope, r))
            for i in range(A_HEADS):
                phase[8 + i].append((neg_max, i))
            for p, d in enumerate(DIAG):
                phase[FIRST[("cf", p)] + 3].append((keys_and_sums, p))
                phase[d - 1].append((diffs, p, 0))
                phase[d + 1].append((take_diagonal, p))
                for lev in range(LEVELS):
                    if lev + 1 < LEVELS:
                        phase[d + lev].append((diffs, p, lev + 1))
                    phase[d + lev].append((operands, p, lev))
                    phase[d + lev + 2].append((take_level, p, lev))
                phase[d + LEVELS - 1].append((block_diffs, p))
                phase[d + LEVELS].append((decayed, p))
                phase[d + LEVELS + 3].append((states, p))
                phase[d + LEVELS + 5].append((head_scaled, p))
            for i in range(A_HEADS):
                phase[8 + i].append((normalise, i))
            for j in range(4):
                phase[12 + 2 * j].append((attn_out, j))
            phase[20].append((spatial_mask,))
            phase[22].append((layer_norm_stats,))
            phase[22].append((layer_norm_scale,))
            for n in SG_JOBS:
                phase[n + 1].append((gate_product, n))
            for m in range(KT):
                phase[FIRST[("out", 0)] + m + 2].append((sum_squares, m))

            with dve.Fori(0, DEPTH) as layer:
                steps[0] = 0
                dve.tensor_copy(VC48, VL[:, layer, :]).then_inc(vecs_ready, 1)
                dve.memset(VB[64:128, 0, :], 0.0).then_inc(first_zero, 1)
                dve.wait_ge(vecs_ready, 1)
                dve.wait_ge(rstd_ready, 1)
                for k in range(KT + 1):
                    if k < KT:
                        if k >= 4:
                            dve.wait_ge(h_lo_pool if k % 2 else h_lo_vec, k // 2 - 1)
                        dve.scalar_tensor_tensor(out=full(k), in0=XT[:, k, :], scalar=ng[:, k:k + 1],
                                                 in1=RS[:, :], op0=ALU.mult, op1=ALU.mult).then_inc(full_ready, 1)
                    if k % 2:
                        dve.wait_ge(h_hi, k)
                        dve.tensor_tensor(out=HL[:, k - 1, :], in0=full(k - 1), in1=HH[:, k - 1, :].bitcast(f32),
                                          op=ALU.subtract).then_inc(h_lo_vec, 1)
                split_lo(1)
                dve.wait_ge(side_in, 16 * 5)
                chained(dve.tensor_scalar(NSK, SK, -1.0, None, ALU.mult))
                for n in range(NJ + 4):
                    split = n < NJ and n > 0 and JOBS[n][1] == 0 and JOBS[n][0] + 1 < NU
                    merging = n < NJ and JOBS[n][0] >= UNITS.index(("merge", 0)) - 1
                    if split and merging:
                        split_lo(JOBS[n][0] + 1)
                    for f, *a in phase[n]:
                        f(*a)
                    if split and not merging:
                        split_lo(JOBS[n][0] + 1)
                    if n < NJ:
                        evac(n)
                split_first(2 * layer + 4)
                dve.drain().then_inc(layer_done, 1)
                dve.wait_ge(layer_go, layer + 1)

            dve.wait_ge(e_rstd, 1)
            dve.wait_ge(fg_in, 16)
            banks = PJ + M[0:4]
            for n in range(2 * TB):
                tb, half = divmod(n, 2)
                dve.wait_ge(e_tr, n + 1)
                dve.scalar_tensor_tensor(out=OUT[:, tb, half * T:(half + 1) * T], in0=banks[n % len(banks)][:, :],
                                         scalar=RT[:, tb:tb + 1], in1=FGB[:, half * T:(half + 1) * T],
                                         op0=ALU.mult, op1=ALU.mult).then_inc(e_evac, 1)


_INS = ["x", "positions", "w_in", "b_merge", "w_branch", "w_out", "norm_g", "final_g", "attn_sinks", "sp_w",
        "sp_b", "sp_ln_g", "sp_ln_b", "hgrn_lb", "hgrn_norm_g"]


def kernel(**inputs):
    import numpy as _np
    import concourse.bacc as _bacc
    from concourse import mybir as _mybir
    from concourse.bass_utils import run_bass_kernel_spmd as _run

    nc = _bacc.Bacc("TRN2", target_bir_lowering=False, num_devices=1)
    arrays = {f"in_{n}": _np.ascontiguousarray(inputs[n]) for n in _INS}
    arrays["in_consts"] = constants()
    args = {n[3:]: nc.dram_tensor(n, a.shape, _mybir.dt.from_np(a.dtype), kind="ExternalInput").ap()
            for n, a in arrays.items()}
    o = nc.dram_tensor("out_0", (1, T, D), _mybir.dt.float32, kind="ExternalOutput").ap()
    build(nc, out=o, **args)
    return _run(nc, [arrays], core_ids=[0]).results[0]["out_0"]
```

```python
from contextlib import ExitStack

import numpy as np
import concourse.bass as bass
from concourse import mybir

DEPTH, T, D = 2, 512, 1024
P = 128
KT = D // P
TB = T // P
A_HEADS, HD = 8, 64
EPS = 1e-6
ROPE_THETA = 10000.0
MASK_VALUE = -1e30
AQ, AK, AV, AG, BU, BV, BG, CQ, CF, CI, CG, MG = (
    int(v) for v in np.cumsum([0, 512, 128, 128, 512, 512, 512, 512, 512, 512, 512, 512]))
UC = 256
KB = 1024

UNITS = ([("q", 0), ("q", 1), ("k", 0), ("v", 0)]
         + [(k, p) for p in range(2) for k in ("cf", "cq", "ci")]
         + [("bv", 0), ("bv", 1), ("ag", 0), ("ag", 1), ("bu", 0), ("bu", 1)]
         + [("bg", 0), ("bg", 1), ("cg", 0), ("cg", 1)]
         + [(k, p * 3 + n) for p in range(4) for n in range(3) for k in ("merge", "mix")]
         + [("out", o) for o in range(4)])
NU = len(UNITS)
JOBS = [(u, t) for u in range(NU) for t in range(1 if UNITS[u][0] in ("k", "v") else 2)]
NJ = len(JOBS)
KIND = [UNITS[u][0] for u, _ in JOBS]
FIRST = {UNITS[u]: n for n, (u, t) in enumerate(JOBS) if t == 0}
JOBS_TO = [max(n for n, (v, _) in enumerate(JOBS) if v == u) + 1 for u in range(NU)]
BY_VECTOR = ("cf", "cq", "ag", "bu", "bg", "cg", "merge", "mix", "out")
EVAC_NO = []
for _k in KIND:
    _e = "v" if _k in BY_VECTOR else "a"
    EVAC_NO.append((_e, 1 + sum(e == _e for e, _ in EVAC_NO)))
SG_JOBS = [n for n in range(NJ) if KIND[n] in ("ag", "bu", "bg", "cg")]
GATE_JOBS = [n for n in SG_JOBS if KIND[n] != "bu"]
BRANCH = {"ag": 0, "bg": 1, "cg": 2}
LEVELS = 7
DIAG = (12, 25)
LATE = {0: 2, 1: 2, 3: 4, 4: 5}
ROPE_AT = (2, 3, 3, 4, 5)
E_POOL, E_VEC, E_OUT = (3, 7), (0, 1, 2, 4, 5, 6), (0, 1, 2, 3, 4, 5, 7, 6)
NJP = 3
WB, RB = 2, 3
assert NU % WB == 0 and NU % RB == 0


def constants():
    c = np.zeros((P, P + 16 * LEVELS + 8), np.float32)
    masks = c[:, P:P + 16 * LEVELS].view(np.uint8)
    c[:, 0:P] = np.eye(P)
    for lev in range(LEVELS):
        s = 64 >> lev
        for i in range(P):
            if i % (2 * s) < s:
                b = i // (2 * s)
                masks[i, 64 * lev + b * s:64 * lev + (b + 1) * s] = 1
    o = P + 16 * LEVELS
    freq = np.float32(ROPE_THETA) ** (-np.arange(0, HD, 2, dtype=np.float32) / np.float32(HD))
    c[:, o] = np.tile(freq, P // (HD // 2))
    c[:, o + 1] = np.where(np.arange(P) % HD < HD // 2, -2.0, 2.0)
    return c


def build(nc, x, positions, w_in, b_merge, w_branch, w_out, norm_g, final_g, attn_sinks, sp_w, sp_b,
          sp_ln_g, sp_ln_b, hgrn_lb, hgrn_norm_g, consts, out):
    f32, f32r, i32 = mybir.dt.float32, mybir.dt.float32r, mybir.dt.int32
    ALU = mybir.AluOpType
    ACT = mybir.ActivationFunctionType
    AX = mybir.AxisListType.X
    SCALE = HD ** -0.5
    NC_ = consts.shape[1]

    ctx = ExitStack()
    with ctx:
        base = [-(-nc.sbuf_base // 32) * 32]

        def region(kib):
            at = base[0]
            base[0] += int(kib * KB)
            return at

        def at(name, shape, offset, dt=f32):
            return nc.alloc_sbuf_tensor_at(name, shape, dt, offset=offset)

        XT = at("xT", [P, KT, T], region(16))
        HH = at("h_hi", [P, KT, T], r_hh := region(16), f32r)
        HL = at("h_lo", [P, KT, T], region(16), f32r)
        r_raw = region(8 * RB)
        RAW = at("w_raw", [P, RB, KT * UC], r_raw)
        WLO = at("w_lo", [P, RB, KT * UC], r_raw, f32r)
        WHI = at("w_hi", [P, WB, KT * UC], region(8 * WB), f32r)
        r_brh, r_brl = region(24), region(24)
        BRH = at("branch_hi", [P, 3, 4, T], r_brh, f32r)
        BRL = at("branch_lo", [P, 3, 4, T], r_brl, f32r)
        OX = at("branch_out", [P, 3, 4, T], r_brh)
        r_ob, r_oc3 = r_brh + 8 * KB, r_brh + 22 * KB
        SPW = at("sp_w_rows", [P, 8, P], r_ob)
        LNG = at("ln_g", [P, T], r_ob + 4 * KB)
        LNB = at("ln_b", [P, T], r_ob + 6 * KB)
        SPB = at("sp_b_rows", [P, 4, P], r_oc3)
        PR = at("probs", [P, 2, TB, P], r_brl)
        VF = at("v_a_features", [P, T], r_brl)
        VA = at("v_a", [P, TB, P], r_brl + 4 * KB)
        KP = at("k_rot", [P, T], r_brl + 6 * KB)
        BC = [at(f"decay_cum{p}", [P, 2, T], r_brl + (8 + 8 * p) * KB) for p in range(2)]
        KK = [at(f"key_c{p}", [P, 2, T], r_brl + (12 + 8 * p) * KB) for p in range(2)]
        r_scr = region(40)
        YH = at("y_hi", [P, KT, T], r_scr, f32r)
        YL = at("y_lo", [P, KT, T], r_scr + 16 * KB, f32r)
        GM = at("merge_gate", [P, 2, 2, T], r_scr + 32 * KB)
        XTOK = at("x_tokens", [P, TB, D], r_scr)
        QP = at("q_rot", [P, 4, T], r_scr)
        GV = at("gelu_v", [P, TB, T], r_scr)
        PT = at("probsT", [P, 2, T], r_scr + 8 * KB)
        WT = at("sp_wT", [P, 8, P], r_scr + 8 * KB)
        QC = [at(f"query_c{p}", [P, 2, T], r_scr + (12 + 4 * p) * KB) for p in range(2)]
        VC = at("v_c", [P, TB, T], r_scr + 20 * KB)
        XL = [at(f"level_ops{b}", [P, 2 * T], r_scr + (28 + 4 * b) * KB) for b in range(2)]
        KHT = at("k_hatT", [P, 2, 3, P], r_scr + 36 * KB)
        VB = at("v_a_even", [P, TB, P], r_scr + 36 * KB)
        E = [at(f"decay{b}", [P, 2 * T], region(4)) for b in range(2)]
        SS = at("sum_sq", [P, T], base[0] - 2 * KB)
        QS = at("q_halves_swapped", [P, 3, T], base[0] - 8 * KB)
        r_at = region(4)
        AT = at("attnT", [P, 2, T], r_at)
        R1 = at("rope_cos", [P, T], r_at)
        R2 = at("rope_sin", [P, T], r_at + 2 * KB)
        TP = at("product", [P, 2, T], r_at)
        ST = at("state", [P, 2, 3, P], region(3))
        r_sg = region(4)
        SG = at("gate", [P, 2, T], r_sg)
        QR = at("q_raw", [P, 3, T], r_sg)
        TT = at("full", [P, 2, T], r_tt := region(4))
        KS = at("k_groups_swapped", [P, T], r_tt + 2 * KB)
        CST = at("consts", [P, NC_], region(NC_ * 4 / KB))
        ONE = at("ones", [P, P], region(0.5))
        RS = at("rstd", [P, T], region(2))
        COS = at("cos", [P, T], region(2))
        SIN = at("sin", [P, T], region(2))
        base[0] = -(-base[0] // 32) * 32
        small = at("small", [P, 250], region(1000 / KB))
        assert DEPTH == 2
        assert base[0] <= nc.sbuf_usable_end, (base[0], nc.sbuf_usable_end)
        VL = small[:, 0:96].rearrange("p (l c) -> p l c", l=2)
        VC48 = small[:, 96:144]
        SK, NSK = small[:, 152:160], small[:, 160:168]
        MX = small[:, 168:172]
        NM = small[:, 172:180].rearrange("p (b t) -> p b t", b=2)
        SM = small[:, 180:188].rearrange("p (b t) -> p b t", b=2)
        ES = small[:, 188:196].rearrange("p (b t) -> p b t", b=2)
        DN = small[:, 196:200]
        RD = small[:, 200:204]
        BS = small[:, 204:228].rearrange("p (b s) -> p b s", b=4)
        MV = small[:, 228:236].rearrange("p (b s) -> p b s", b=4)
        RL = small[:, 236:240]
        EP = small[:, 240:241]
        PIH = small[:, 241:242]
        RT = small[:, 242:246]
        VR = at("vec_rows", [96, P], r_brl)
        LBT = at("lb_work", [P, 64], r_brl + 1 * KB)
        POSI = at("pos_int", [P, T], r_brh, i32)
        ANG = at("angle", [P, T], r_brh + 2 * KB)
        TRN = at("turns", [P, T], r_brh + 4 * KB)
        SH = at("sin_half", [P, T], r_brh + 6 * KB)
        CH = at("cos_half", [P, T], r_brh + 8 * KB)
        OUT = at("out_tokens", [P, TB, D], r_hh)
        FGB = at("final_g_rows", [P, D], r_hh + 16 * KB)

        ID = CST[:, 0:P]
        FREQ, SIGN2 = (CST[:, P + 16 * LEVELS + c:P + 16 * LEVELS + c + 1] for c in (0, 1))

        def mask(lev):
            return CST[:, P + 16 * lev:P + 16 * (lev + 1)].bitcast(mybir.dt.uint8)

        ng = VC48[:, 0:8]
        bm = VC48[:, 8:32]
        hng, lb, oml, noml = (VC48[:, c:c + 4] for c in (32, 36, 40, 44))

        PJ = [ctx.enter_context(nc.psum_tensor(f"pj{b}", [P, T], f32)) for b in range(NJP)]
        M = [ctx.enter_context(nc.psum_tensor(f"mx{b}", [P, T], f32)) for b in range(5)]

        def sem(name):
            return ctx.enter_context(nc.semaphore(name))

        layer_sems = []

        def lsem(name):
            layer_sems.append(sem(name))
            return layer_sems[-1]

        layer_done = lsem("layer_done")
        raw_in = [lsem(f"raw_in{b}") for b in range(RB)]
        side_in = lsem("side_in")
        w_hi, w_lo, w_lo_vec = lsem("w_hi"), lsem("w_lo"), lsem("w_lo_vec")
        pj_done = lsem("pj_done")
        act_evac, vec_evac = lsem("act_evac"), lsem("vec_evac")
        norm_sum, rstd_ready = lsem("norm_sum"), lsem("rstd_ready")
        vT_done, va_ready = lsem("vT_done"), lsem("va_ready")
        clamped, vb_ready, sg_ready, gm_ready = (
            lsem(n) for n in ("clamped", "vb_ready", "sg_ready", "gm_ready"))
        vec_step, act_step, pool_step = lsem("vec_step"), lsem("act_step"), lsem("pool_step")
        vecs_ready = lsem("vecs_ready")
        rope_done, k_swapped = lsem("rope_done"), lsem("k_swapped")
        scores_done, negmax_ready, exp_done = lsem("scores_done"), lsem("negmax_ready"), lsem("exp_done")
        probs_ready, pT_done, pT_evac, pv_done = lsem("probs_ready"), lsem("pT_done"), lsem("pT_evac"), lsem("pv_done")
        oa_evac, first_zero = lsem("oa_evac"), lsem("first_zero")
        sig_ready, logf_ready = lsem("sig_ready"), lsem("logf_ready")
        c_keys = lsem("c_keys")
        diff_done, decay_ready, ops_ready = lsem("diff_done"), lsem("decay_ready"), lsem("ops_ready")
        lev_done, at_evac = lsem("lev_done"), lsem("at_evac")
        khat_ready, khT_done, khT_evac = lsem("khat_ready"), lsem("khT_done"), lsem("khT_evac")
        upd_done, state_ready, oc_done = lsem("upd_done"), lsem("state_ready"), lsem("oc_done")
        oc_evac, ocn_done, oc_rstd, oc_ready = lsem("oc_evac"), lsem("ocn_done"), lsem("oc_rstd"), lsem("oc_ready")
        wT_done, wT_evac, wT_ready = lsem("wT_done"), lsem("wT_evac"), lsem("wT_ready")
        ln_stats, ln_rstd, ln_scaled, gv_ready = lsem("ln_stats"), lsem("ln_rstd"), lsem("ln_scaled"), lsem("gv_ready")
        sv_done = lsem("sv_done")
        gated, br_hi, br_lo = lsem("gated"), lsem("br_hi"), lsem("br_lo")
        y_full, y_hi, y_lo = lsem("y_full"), lsem("y_hi"), lsem("y_lo")
        sq_ready, ss_added = lsem("sq_ready"), lsem("ss_added")
        first_num, last_num = layer_sems[0].num, layer_sems[-1].num
        assert last_num - first_num + 1 == len(layer_sems)
        layer_go, layer_seen = sem("layer_go"), sem("layer_seen")
        first_in = [sem(f"first_in{u}") for u in range(RB)]
        xg_hi, xg_lo = sem("xg_hi"), sem("xg_lo")
        first_hi, first_lo, first_lo_vec = sem("first_hi"), sem("first_lo"), sem("first_lo_vec")
        ss_ready = sem("ss_ready")
        x_in = [sem(f"x_in{j}") for j in range(KT // 2)]
        vec_in, cst_in, pos_in = sem("vec_in"), sem("cst_in"), sem("pos_in")
        fill_done, xT_done, xT_evac = sem("fill_done"), sem("xT_done"), sem("xT_evac")
        pro_step = sem("pro_step")
        p_half = sem("p_half")
        p_vec, p_act, p_sq, p_ss = sem("p_vec"), sem("p_act"), sem("p_sq"), sem("p_ss")
        vecT_done, p_diff, p_exp, p_trig, p_sin = sem("vecT_done"), sem("p_diff"), sem("p_exp"), sem("p_trig"), sem("p_sin")
        fg_in = sem("fg_in")
        e_sum, e_rstd, e_tr, e_scaled = (sem(n) for n in ("e_sum", "e_rstd", "e_tr", "e_scaled"))
        e_evac, e_evac_pool, out_sent = sem("e_evac"), sem("e_evac_pool"), sem("out_sent")

        def out_bank(n):
            return (M[0:4] + PJ + M[4:])[n]

        def bank_of(n):
            return M[n] if n < 2 else PJ[n % NJP]

        def evacuated(eng, n):
            which, value = EVAC_NO[n]
            eng.wait_ge(act_evac if which == "a" else vec_evac, value)

        def unit_load(layer, u):
            kind, i = UNITS[u]

            def w(col, n):
                return w_in[layer, :, col:col + n].rearrange("(k p) c -> p k c", p=P)

            buf = RAW[:, u % RB, :].rearrange("p (k c) -> p k c", c=UC)
            if kind == "mix":
                p, n = divmod(i, 3)
                rows = w_branch[layer, n, :, p * UC:(p + 1) * UC]
                return (buf[:, 0:4, :], rows.rearrange("(k p) c -> p k c", p=P))
            if kind == "out":
                return (buf, w_out[layer, :, i * UC:(i + 1) * UC].rearrange("(k p) c -> p k c", p=P))
            if kind in ("k", "v"):
                return (buf[:, :, 0:P], w(AK if kind == "k" else AV, P))
            if kind == "merge":
                p, n = divmod(i, 3)
                return (buf, w(MG + n * D + p * UC, UC))
            c0 = {"q": AQ, "ag": AG, "cf": CF, "cq": CQ, "ci": CI, "bv": BV, "bu": BU, "bg": BG, "cg": CG}[kind]
            return (buf, w(c0 + i * UC, UC))

        def part(buf, u, half):
            kind = UNITS[u][0]
            kn, cn = (4 if kind == "mix" else KT), (P if kind in ("k", "v") else UC)
            return buf.rearrange("p (k c) -> p k c", c=UC)[:, half * kn // 2:(half + 1) * kn // 2, 0:cn]

        def loaded(u):
            return 16 * (u // RB)

        def load_weights(eng, layer, u):
            eng.dma_start(*unit_load(layer, u)).then_inc(first_in[u], 16)

        def x_bank(k):
            return (M[2:] + PJ)[k % 6]

        block = ctx.enter_context(nc.Block())

        @block.sync
        def _(sp):
            sp.dma_start(CST[:, :], consts[:, :]).then_inc(cst_in, 16)
            for j in range(KT // 2):
                c = slice(2 * j * P, 2 * (j + 1) * P)
                sp.dma_start(XTOK[:, :, c], x[0, :, c].rearrange("(b p) d -> p b d", p=P)).then_inc(x_in[j], 16)
                if j == 1:
                    load_weights(sp, 0, 0)
            for u in range(1, RB):
                load_weights(sp, 0, u)
            sp.wait_ge(p_trig, 1)
            with sp.Fori(0, DEPTH) as layer:
                sp.wait_ge(layer_go, layer + 1)
                sp.sem_inc(layer_seen, 1)
                sp.dma_start(SPW[:, :, :], sp_w[layer].rearrange("g t s -> t g s")).then_inc(side_in, 16)
                sp.dma_start(LNG[:, :], sp_ln_g[layer].partition_broadcast(P)).then_inc(side_in, 16)
                sp.dma_start(LNB[:, :], sp_ln_b[layer].partition_broadcast(P)).then_inc(side_in, 16)
                for g in range(2):
                    sp.dma_start(SPB[g * HD:(g + 1) * HD, :, :],
                                 sp_b[layer].rearrange("(c g) t -> g c t", g=2)[g].partition_broadcast(HD))\
                      .then_inc(side_in, 16)
                sp.dma_start(SK, attn_sinks[layer].partition_broadcast(P)).then_inc(side_in, 16)
                for u in range(RB, NU):
                    sp.wait_ge(pj_done, JOBS_TO[u - RB])
                    sp.dma_start(*unit_load(layer, u)).then_inc(raw_in[u % RB], 16)
                for u in range(RB):
                    sp.wait_ge(pj_done, JOBS_TO[NU - RB + u])
                    load_weights(sp, DEPTH - 1, u)
                sp.drain().then_inc(layer_done, 1)
            sp.wait_ge(xg_lo, (DEPTH + 1) * KT)
            sp.dma_start(FGB[:, :], final_g.partition_broadcast(P)).then_inc(fg_in, 16)
            for n in E_OUT:
                half, tb = divmod(n, TB)
                c = slice(half * T, (half + 1) * T)
                if n in E_POOL:
                    sp.wait_ge(e_evac_pool, E_POOL.index(n) + 1)
                else:
                    sp.wait_ge(e_evac, E_VEC.index(n) + 1)
                sp.dma_start(out[0, tb * P:(tb + 1) * P, c], OUT[:, tb, c]).then_inc(out_sent, 16)
            sp.wait_ge(out_sent, 16 * 2 * TB)

        @block.tensor
        def _(pe):
            pe.wait_ge(cst_in, 16)
            for k in range(KT):
                if k % 2 == 0:
                    pe.wait_ge(x_in[k // 2], 16)
                if k >= 6:
                    pe.wait_ge(xT_evac, k - 5)
                for tb in range(TB):
                    last = pe.transpose(x_bank(k)[:, tb * P:(tb + 1) * P], XTOK[:, tb, k * P:(k + 1) * P], ID)
                last.then_inc(xT_done, 1)
                if k == 1:
                    pe.wait_ge(vec_in, 16 * 4)
                    pe.transpose(M[0][:, 0:80], VR[0:80, :], CST[0:80, 0:80]).then_inc(vecT_done, 1)
            pe.wait_ge(fill_done, 1)

            def operands(n):
                u, t = JOBS[n]
                kind, i = UNITS[u]
                wh = WHI[:, u % WB, :].rearrange("p (k c) -> p k c", c=UC)
                wl = WLO[:, u % RB, :].rearrange("p (k c) -> p k c", c=UC)
                if kind == "mix":
                    return bank_of(n), wh, wl, BRH[:, i % 3], BRL[:, i % 3], 4
                if kind == "out":
                    return bank_of(n), wh, wl, YH, YL, KT
                return bank_of(n), wh, wl, HH, HL, KT

            def claim(n, layer):
                u, t = JOBS[n]
                if t == 0 and u < 2:
                    pe.wait_ge(first_lo, 2 * layer + u + 1)
                    pe.wait_ge(first_lo_vec, 2 * layer + u + 1)
                elif t == 0:
                    pe.wait_ge(w_lo, u - 1)
                    pe.wait_ge(w_lo_vec, u - 1)
                if n >= NJP + 2:
                    evacuated(pe, n - NJP)

            def three(bank, wh, wl, ah, al, first, final):
                pe.matmul(bank, wh, ah, start=first, stop=False)
                pe.matmul(bank, wh, al, start=False, stop=False)
                return pe.matmul(bank, wl, ah, start=False, stop=final)

            def project_both(n, layer):
                claim(n, layer)
                claim(n + 1, layer)
                for k in range(KT):
                    if n == 0:
                        pe.wait_ge(xg_lo, layer * KT + k + 1)
                        if k == KT - 1:
                            pe.wait_ge(layer_go, layer + 1)
                    else:
                        pe.wait_ge(y_lo, k + 1)
                    for t in range(2):
                        bank, wh, wl, ah, al, kn = operands(n + t)
                        c = slice(t * P, (t + 1) * P)
                        last = three(bank[:, :], wh[:, k, c], wl[:, k, c], ah[:, k, :], al[:, k, :],
                                     k == 0, k == KT - 1)
                        if k == KT - 1:
                            last.then_inc(pj_done, 1)

            def project(n, layer):
                claim(n, layer)
                u, t = JOBS[n]
                kind, i = UNITS[u]
                bank, wh, wl, ah, al, kn = operands(n)
                if kind in ("ci", "bv"):
                    for b in range(2):
                        tok = slice((2 * t + b) * P, (2 * t + b + 1) * P)
                        for k in range(KT):
                            last = three(bank[:, b * UC:(b + 1) * UC], ah[:, k, tok], al[:, k, tok],
                                         wh[:, k, :], wl[:, k, :], k == 0, k == KT - 1)
                    last.then_inc(pj_done, 1)
                    return
                if kind == "mix" and i < 3 and t == 0:
                    pe.wait_ge(br_lo, 4 * (i + 1))
                c = slice(t * P, (t + 1) * P)
                for k in range(kn):
                    last = three(bank[:, :], wh[:, k, c], wl[:, k, c], ah[:, k, :], al[:, k, :],
                                 k == 0, k == kn - 1)
                last.then_inc(pj_done, 1)

            def transpose_values():
                evacuated(pe, FIRST[("v", 0)])
                for tb in range(TB):
                    last = pe.transpose(M[2][:, tb * P:(tb + 1) * P], VF[:, tb * P:(tb + 1) * P], ID)
                last.then_inc(vT_done, 1)

            def scores(i):
                j, half = divmod(i, 2)
                if i == 0:
                    pe.wait_ge(rope_done, 5)
                else:
                    pe.wait_ge(exp_done, i)
                if i == 1:
                    pe.wait_ge(k_swapped, 1)
                d = slice(half * HD, (half + 1) * HD)
                keys = KP if i // 4 == half else KS
                for tb in range(TB):
                    q0 = tb * P
                    pe.matmul(M[0][64:128, q0:q0 + P], QP[d, j, q0 + 64:q0 + P], keys[d, q0:q0 + P],
                              start=True, stop=True)
                    last = pe.matmul(M[0][0:64, q0:q0 + 64], QP[d, j, q0:q0 + 64], keys[d, q0:q0 + 64],
                                     start=True, stop=True)
                    if tb > 0:
                        last = pe.matmul(M[0][0:64, q0 + 64:q0 + P], QP[d, j, q0:q0 + 64], keys[d, q0 - 64:q0],
                                         start=True, stop=True)
                last.then_inc(scores_done, 1)

            def transpose_probs(i):
                pe.wait_ge(probs_ready, i + 1)
                if i >= 1:
                    pe.wait_ge(pT_evac, i)
                for tb in range(TB):
                    last = pe.transpose(M[1][:, tb * P:(tb + 1) * P], PR[:, i % 2, tb, :], ID)
                last.then_inc(pT_done, 1)

            def attend(i):
                j, half = divmod(i, 2)
                pe.wait_ge(pT_evac, i + 1)
                pe.wait_ge(first_zero, 1)
                pe.wait_ge(vb_ready, 1)
                if half == 0 and j >= 1:
                    pe.wait_ge(oa_evac, j)
                v = slice(i // 4 * HD, (i // 4 + 1) * HD)
                o = slice(half * HD, (half + 1) * HD)
                for tb in range(TB):
                    q0 = tb * P
                    pe.matmul(M[2][o, q0:q0 + 64], VB[:, tb, v],
                              PT[:, i % 2, q0:q0 + 64], start=True, stop=True)
                    last = pe.matmul(M[2][o, q0 + 64:q0 + P], VA[:, tb, v],
                                     PT[:, i % 2, q0 + 64:q0 + P], start=True, stop=True)
                last.then_inc(pv_done, 1)

            def diagonal(p):
                evacuated(pe, FIRST[("cq", p)] + 1)
                pe.wait_ge(c_keys, p + 1)
                if p == 1:
                    pe.wait_ge(oc_rstd, 1)
                for hh in range(2):
                    for tb in range(TB):
                        b = slice(tb * P, (tb + 1) * P)
                        last = pe.matmul(M[3 + hh][:, b], KK[p][:, hh, b], QC[p][:, hh, b], start=True, stop=True)
                last.then_inc(lev_done, 1)

            def level(p, lev):
                s = 64 >> lev
                pe.wait_ge(ops_ready, LEVELS * p + lev + 1)
                pe.wait_ge(at_evac, (LEVELS + 1) * p + max(lev, 1))
                ops = XL[lev % 2]
                for hb in range(2 * TB):
                    blk = ops[:, hb * P:(hb + 1) * P]
                    upper = blk.rearrange("p (b u s) -> p b u s", u=2, s=s)[:, :, 1, :]
                    rows = 64 if lev == 0 else P
                    last = pe.matmul(M[3 + lev % 2][0:rows, hb * 64:(hb + 1) * 64], blk[:, 0:rows], upper,
                                     start=True, stop=True)
                last.then_inc(lev_done, 1)

            def transpose_khat(p):
                pe.wait_ge(khat_ready, p + 1)
                pe.wait_ge(at_evac, (LEVELS + 1) * (p + 1))
                for hh in range(2):
                    for c in range(3):
                        last = pe.transpose(M[3 + hh][:, c * P:(c + 1) * P], KK[p][:, hh, c * P:(c + 1) * P], ID)
                last.then_inc(khT_done, 1)

            def state_updates(p):
                pe.wait_ge(khT_evac, p + 1)
                evacuated(pe, FIRST[("ci", p)] + 1)
                for hh in range(2):
                    h = 2 * p + hh
                    for c in range(3):
                        last = pe.matmul(M[3 + hh][:, c * P:(c + 1) * P], KHT[:, hh, c, :],
                                         VC[:, c, h * P:(h + 1) * P], start=True, stop=True)
                last.then_inc(upd_done, 1)

            def recurrent_out(p):
                pe.wait_ge(state_ready, p + 1)
                for hh in range(2):
                    h = 2 * p + hh
                    for tb in range(TB):
                        b = slice(tb * P, (tb + 1) * P)
                        last = pe.matmul(M[3 + hh][:, b], VC[:, tb, h * P:(h + 1) * P], AT[:, hh, b],
                                         start=True, stop=(tb == 0))
                        if tb > 0:
                            last = pe.matmul(M[3 + hh][:, b], ST[:, hh, tb - 1, :], QC[p][:, hh, b],
                                             start=False, stop=True)
                last.then_inc(oc_done, 1)

            def head_norm(p):
                pe.wait_ge(oc_evac, p + 1)
                for hh in range(2):
                    last = pe.matmul(M[3 + hh][:, :], ONE[:, :], AT[:, hh, :], start=True, stop=True)
                last.then_inc(ocn_done, 1)

            def transpose_spatial():
                pe.wait_ge(side_in, 16 * 6)
                pe.wait_ge(pT_evac, A_HEADS)
                for g in range(8):
                    last = pe.transpose(M[g // 4][:, (g % 4) * P:(g % 4 + 1) * P], SPW[:, g, :], ID)
                last.then_inc(wT_done, 1)

            def spatial(ct):
                if ct == 0:
                    pe.wait_ge(wT_ready, 1)
                    pe.wait_ge(gv_ready, 1)
                    pe.wait_ge(oa_evac, 4)
                if ct == 3:
                    pe.wait_ge(gated, SG_JOBS.index(FIRST[("bu", 0)]) + 1)
                bank = M[ct % 3]
                for g in range(2):
                    for nb in range(TB):
                        c = (2 * ct + g) * HD
                        last = pe.matmul(bank[g * HD:(g + 1) * HD, nb * P:(nb + 1) * P], GV[:, nb, c:c + HD],
                                         WT[:, 2 * ct + g, :], start=True, stop=True)
                last.then_inc(sv_done, 1)

            hooks = {n: [] for n in range(NJ)}
            hooks[FIRST[("v", 0)] + 2].append((transpose_values,))
            for i in range(A_HEADS):
                hooks[10 + i].append((attend, i))
            for i in range(A_HEADS):
                hooks[9 + i].append((transpose_probs, i))
            for i in range(A_HEADS):
                hooks[7 + i].append((scores, i))
            for p, d in enumerate(DIAG):
                hooks[d].append((diagonal, p))
                for lev in range(LEVELS):
                    hooks[d + 1 + lev].append((level, p, lev))
                for step, f in enumerate((transpose_khat, state_updates, recurrent_out, head_norm)):
                    hooks[d + 1 + LEVELS + step].append((f, p))
            hooks[18].append((transpose_spatial,))
            for ct in range(4):
                hooks[25 + ct].append((spatial, ct))

            with pe.Fori(0, DEPTH) as layer:
                for n in range(NJ):
                    if n in (0, FIRST[("out", 0)]):
                        project_both(n, layer)
                    elif n not in (1, FIRST[("out", 0)] + 1):
                        project(n, layer)
                    if n == 0:
                        pe.wait_ge(xT_evac, KT)
                        pe.wait_ge(ss_ready, layer + 1)
                        pe.matmul(M[4][:, :], ONE[:, :], SS[:, :], start=True, stop=True)
                        for tb in range(TB):
                            last = pe.matmul(M[3][:, tb:tb + 1], SS[:, tb * P:(tb + 1) * P], ONE[:, 0:1],
                                             start=True, stop=True)
                        last.then_inc(norm_sum, 1)
                    for f, *a in hooks[n]:
                        f(*a)
                pe.sem_inc(layer_done, 1)

            for n in range(2 * TB):
                half, tb = divmod(n, TB)
                if n == TB:
                    pe.wait_ge(ss_ready, DEPTH + 1)
                    for b in range(TB):
                        last = pe.matmul(M[4][:, b:b + 1], SS[:, b * P:(b + 1) * P], ONE[:, 0:1],
                                         start=True, stop=True)
                    last.then_inc(e_sum, 1)
                if n == 2 * TB - 1:
                    pe.wait_ge(p_act, 1)
                for c in range(4):
                    if tb == 0:
                        pe.wait_ge(xg_hi, DEPTH * KT + 4 * half + c + 1)
                    last = pe.transpose(out_bank(n)[:, c * P:(c + 1) * P],
                                        XT[:, 4 * half + c, tb * P:(tb + 1) * P], ID)
                last.then_inc(e_tr, 1)

        @block.scalar
        def _(act):
            steps = [0]

            def chained(ins):
                steps[0] += 1
                ins.then_inc(act_step, 1)
                act.wait_ge(act_step, steps[0])

            act.dma_start(VR[0:16, :], norm_g.rearrange("l (k p) -> (l k) p", p=P)).then_inc(vec_in, 16)
            act.dma_start(VR[16:64, :], b_merge.rearrange("l n (k p) -> (l n k) p", p=P)).then_inc(vec_in, 16)
            act.dma_start(VR[64:72, :], hgrn_norm_g.rearrange("l (k p) -> (l k) p", p=P)).then_inc(vec_in, 16)
            act.dma_start(VR[72:80, :], hgrn_lb.rearrange("l (k p) -> (l k) p", p=P)).then_inc(vec_in, 16)

            def scaled_hi(k, layer):
                return act.activation(HH[:, k, :], XT[:, k, :], ACT.Copy, scale=VL[:, layer, k:k + 1])

            def split_first(u, value):
                act.wait_ge(first_in[u], value)
                for half in range(2):
                    act.activation(part(WHI[:, u, :], u, half), part(RAW[:, u, :], u, half), ACT.Copy)\
                       .then_inc(first_hi, 1)

            act.wait_ge(p_vec, 1)
            for k in range(KT):
                if k == 2:
                    split_first(0, 16)
                act.wait_ge(xT_done, k + 1)
                act.activation(XT[:, k, :], x_bank(k)[:, :], ACT.Copy).then_inc(xT_evac, 1)
                act.wait_ge(xT_evac, k + 1)
                scaled_hi(k, 0).then_inc(xg_hi, 1)
            split_first(1, 16)
            act.wait_ge(fill_done, 1)
            act.wait_ge(p_half, 1)
            act.activation(SH[:, :], ANG[:, :], ACT.Sin)
            act.activation(CH[:, :], TRN[:, :], ACT.Sin, bias=PIH, scale=-1.0).then_inc(p_sin, 1)
            act.wait_ge(p_diff, 1)
            act.activation(LBT[:, 12:20], LBT[:, 4:12], ACT.Exp).then_inc(p_exp, 1)

            def rsqrt(dst, src, scale):
                chained(act.activation(dst, src, ACT.Ln, bias=EP, scale=scale))
                return act.activation(dst, dst, ACT.Exp, scale=-0.5)

            def split_hi(u, layer):
                if u < RB:
                    act.wait_ge(first_in[u], 16 * (layer + 1))
                else:
                    act.wait_ge(raw_in[u % RB], loaded(u))
                if u >= WB:
                    act.wait_ge(pj_done, JOBS_TO[u - WB])
                for half in range(2):
                    act.activation(part(WHI[:, u % WB, :], u, half), part(RAW[:, u % RB, :], u, half), ACT.Copy)\
                       .then_inc(w_hi, 1)

            def evac(n):
                u, t = JOBS[n]
                kind, i = UNITS[u]
                src = bank_of(n)[:, :]
                done = act_evac
                if kind in BY_VECTOR:
                    return
                act.wait_ge(pj_done, n + 1)
                if kind in ("q", "k"):
                    if n >= 3:
                        act.wait_ge(rope_done, n - 2)
                    for a in range(0, P, HD):
                        b, c = a + HD // 2, a + HD
                        act.activation(QS[a:b, n % 3, :], src[b:c], ACT.Copy)
                        act.activation(QS[b:c, n % 3, :], src[a:b], ACT.Copy)
                    act.activation(QR[:, n % 3, :], src, ACT.Copy).then_inc(done, 1)
                elif kind == "v":
                    act.activation(VF[:, :], src, ACT.Copy).then_inc(done, 1)
                else:
                    if kind == "bv" and i == 0 and t == 0:
                        act.wait_ge(scores_done, A_HEADS)
                    dst, fn = (VC, ACT.Copy) if kind == "ci" else (GV, ACT.Gelu_apprx_tanh)
                    for b in range(2):
                        tb = 2 * t + b
                        last = act.activation(dst[:, tb, i * UC:(i + 1) * UC], src[:, b * UC:(b + 1) * UC], fn,
                                              scale=RT[:, tb:tb + 1])
                    last.then_inc(done, 1)

            def values():
                act.wait_ge(vT_done, 1)
                for b in range(TB):
                    last = act.activation(VA[:, b, :], M[2][:, b * P:(b + 1) * P], ACT.Copy, scale=RT[:, b:b + 1])
                last.then_inc(va_ready, 1)

            def swap_keys():
                act.wait_ge(rope_done, 5)
                for a, b in ((0, HD), (HD, 0)):
                    last = act.activation(KS[a:a + HD, :], KP[b:b + HD, :], ACT.Copy)
                last.then_inc(k_swapped, 1)

            def gate(n):
                s = SG_JOBS.index(n)
                evacuated(act, n)
                fn = ACT.Gelu_apprx_tanh if KIND[n] == "bu" else ACT.Silu
                act.activation(SG[:, s % 2, :], SG[:, s % 2, :], fn).then_inc(sg_ready, 1)

            def merge_gate(n):
                u, t = JOBS[n]
                i = UNITS[u][1]
                p, b = divmod(i, 3)
                c = 8 * b + 2 * p + t
                evacuated(act, n)
                act.activation(GM[:, i % 2, t, :], GM[:, i % 2, t, :], ACT.Sigmoid, bias=bm[:, c:c + 1])\
                   .then_inc(gm_ready, 1)

            def softmax_exp(i):
                if i == 0:
                    act.wait_ge(side_in, 16 * 6)
                act.wait_ge(negmax_ready, i + 1)
                if i >= 2:
                    act.wait_ge(pT_done, i - 1)
                for tb in range(TB):
                    act.activation(PR[:, i % 2, tb, :], M[0][:, tb * P:(tb + 1) * P], ACT.Exp,
                                   bias=NM[:, i % 2, tb:tb + 1], scale=SCALE, accum_out=SM[:, i % 2, tb:tb + 1])
                act.activation(ES[:, i % 2, :], NM[:, i % 2, :], ACT.Exp, bias=SK[:, i:i + 1])\
                   .then_inc(exp_done, 1)

            def probsT_out(i):
                act.wait_ge(pT_done, i + 1)
                if i >= 2:
                    act.wait_ge(pv_done, i - 1)
                act.activation(PT[:, i % 2, :], M[1][:, :], ACT.Copy).then_inc(pT_evac, 1)

            def forget(p):
                act.wait_ge(clamped, p + 1)
                act.activation(KK[p][:, :, :], BC[p][:, :, :], ACT.Sigmoid).then_inc(sig_ready, 1)
                act.wait_ge(sig_ready, p + 1)
                for hh in range(2):
                    h = 2 * p + hh
                    last = act.activation(BC[p][:, hh, :], KK[p][:, hh, :], ACT.Ln,
                                          bias=lb[:, h:h + 1], scale=oml[:, h:h + 1])
                last.then_inc(logf_ready, 1)

            def decay_exp(p, lev):
                act.wait_ge(diff_done, (LEVELS + 1) * p + lev + 1)
                act.activation(E[lev % 2][:, :], E[lev % 2][:, :], ACT.Exp).then_inc(decay_ready, 1)

            def block_exp(p):
                act.wait_ge(diff_done, (LEVELS + 1) * (p + 1))
                act.wait_ge(ops_ready, LEVELS * (p + 1))
                act.activation(E[1][:, 0:6 * P], E[1][:, 0:6 * P], ACT.Exp)
                act.activation(E[0][:, :], BC[p][:, :, :].rearrange("p h t -> p (h t)"), ACT.Exp)\
                   .then_inc(decay_ready, 1)

            def khatT_out(p):
                act.wait_ge(khT_done, p + 1)
                if p == 1:
                    act.wait_ge(upd_done, 1)
                for hh in range(2):
                    last = act.activation(KHT[:, hh, :, :], M[3 + hh][:, 0:3 * P].rearrange("p (c d) -> p c d", c=3),
                                          ACT.Copy)
                last.then_inc(khT_evac, 1)

            def recurrent_evac(p):
                act.wait_ge(oc_done, p + 1)
                for hh in range(2):
                    act.activation(OX[:, 2, 2 * p + hh, :], M[3 + hh][:, :], ACT.Copy)
                    last = act.activation(AT[:, hh, :], M[3 + hh][:, :], ACT.Square)
                last.then_inc(oc_evac, 1)

            def head_rstd(p):
                act.wait_ge(ocn_done, p + 1)
                for hh in range(2):
                    last = act.activation(AT[:, hh, :], M[3 + hh][:, :], ACT.Ln, bias=EP, scale=1.0 / P)
                chained(last)
                act.activation(AT[:, :, :], AT[:, :, :], ACT.Exp, scale=-0.5).then_inc(oc_rstd, 1)

            def spatialT_out():
                act.wait_ge(wT_done, 1)
                act.wait_ge(pv_done, A_HEADS)
                for b in range(2):
                    last = act.activation(WT[:, 4 * b:4 * b + 4, :],
                                          M[b][:, :].rearrange("p (g t) -> p g t", g=4), ACT.Copy)
                last.then_inc(wT_evac, 1)

            def ln_rsqrt():
                act.wait_ge(ln_stats, 1)
                rsqrt(RL, MV[:, :, 1], 1.0).then_inc(ln_rstd, 1)

            def branch_hi(n):
                gi = GATE_JOBS.index(n)
                act.wait_ge(gated, SG_JOBS.index(n) + 1)
                kind = KIND[n]
                ct = n - FIRST[(kind, 0)]
                act.activation(BRH[:, BRANCH[kind], ct, :], TT[:, gi % 2, :], ACT.Copy).then_inc(br_hi, 1)

            def y_high(m):
                act.wait_ge(y_full, m + 1)
                act.activation(YH[:, m, :], TT[:, m % 2, :], ACT.Copy).then_inc(y_hi, 1)

            def next_x(m):
                evacuated(act, FIRST[("out", 0)] + m)
                if m >= 2:
                    act.wait_ge(ss_added, m - 1)
                act.activation(TP[:, m % 2, :], XT[:, m, :], ACT.Square).then_inc(sq_ready, 1)
                scaled_hi(m, DEPTH - 1).then_inc(xg_hi, 1)

            def token_rstd():
                act.wait_ge(norm_sum, 1)
                act.activation(RT, M[3][:, 0:TB], ACT.Ln, bias=EP, scale=1.0 / D)
                chained(act.activation(RS[:, :], M[4][:, :], ACT.Ln, bias=EP, scale=1.0 / D))
                act.activation(RT, RT, ACT.Exp, scale=-0.5)
                act.activation(RS[:, :], RS[:, :], ACT.Exp, scale=-0.5).then_inc(rstd_ready, 1)
                act.wait_ge(rstd_ready, 1)

            phase = {n: [] for n in range(NJ + 4)}
            phase[1].append((token_rstd,))
            phase[ROPE_AT[4] + 2].append((swap_keys,))
            phase[FIRST[("v", 0)] + 3].append((values,))
            for i in range(A_HEADS):
                phase[10 + i].append((probsT_out, i))
                phase[8 + i].append((softmax_exp, i))
            for p, d in enumerate(DIAG):
                phase[FIRST[("cf", p)] + 2].append((forget, p))
                for lev in range(LEVELS):
                    phase[d - 1 + lev].append((decay_exp, p, lev))
                phase[d + LEVELS].append((block_exp, p))
                phase[d + LEVELS + 2].append((khatT_out, p))
                phase[d + LEVELS + 4].append((recurrent_evac, p))
                phase[d + LEVELS + 5].append((head_rstd, p))
            phase[19].append((spatialT_out,))
            phase[22].append((ln_rsqrt,))
            for n in range(NJ):
                if n in SG_JOBS:
                    phase[n + 1].append((gate, n))
                if KIND[n] == "merge":
                    phase[n + 1].append((merge_gate, n))
            for n in GATE_JOBS:
                phase[n + 2].append((branch_hi, n))
            for m in range(KT):
                phase[FIRST[("mix", 3 * (m // 2) + 2)] + 1 + m % 2].append((y_high, m))
                phase[FIRST[("out", 0)] + m + 1].append((next_x, m))

            with act.Fori(0, DEPTH) as layer:
                act.wait_ge(layer_go, layer + 1)
                act.sem_inc(layer_seen, 1)
                steps[0] = 0
                for n in range(NJ + 4):
                    if n < NJ and n > 0 and JOBS[n][1] == 0 and JOBS[n][0] + 1 < NU:
                        split_hi(JOBS[n][0] + 1, layer)
                    for late, when in LATE.items():
                        if when == n:
                            evac(late)
                    for f, *a in phase[n]:
                        f(*a)
                    if n < NJ and n not in LATE:
                        evac(n)
                    if n == JOBS_TO[NU - 2]:
                        split_first(0, 16 * (layer + 2))
                act.wait_ge(pj_done, NJ)
                split_first(1, 16 * (layer + 2))
                act.drain().then_inc(layer_done, 1)

            act.wait_ge(e_sum, 1)
            act.activation(RT, M[4][:, 0:TB], ACT.Sqrt, bias=EP, scale=1.0 / D).then_inc(p_act, 1)
            for n in E_POOL:
                half, tb = divmod(n, TB)
                act.wait_ge(e_rstd, 1)
                act.wait_ge(e_tr, n + 1)
                act.activation(OUT[:, tb, half * T:(half + 1) * T], out_bank(n)[:, :], ACT.Copy,
                               scale=RT[:, tb:tb + 1]).then_inc(e_scaled, 1)

        @block.gpsimd
        def _(pool):
            pool.dma_start(POSI[:, :], positions[0].partition_broadcast(P)).then_inc(pos_in, 16)
            pool.memset(ONE[:, :], 1.0)
            pool.memset(EP, EPS)
            pool.memset(PIH, float(np.pi / 2)).then_inc(fill_done, 1)
            pool.sem_inc(layer_go, 1)

            def sub(dst, full, hi):
                return pool.tensor_tensor(out=dst, in0=full, in1=hi.bitcast(f32), op=ALU.subtract)

            def split_lo(u):
                pool.wait_ge(w_hi, 2 * (u - 1) - 1)
                sub(part(WLO[:, u % RB, :], u, 0), part(RAW[:, u % RB, :], u, 0), part(WHI[:, u % WB, :], u, 0))\
                    .then_inc(w_lo, 1)

            def split_first(u, value):
                pool.wait_ge(first_hi, value)
                sub(part(WLO[:, u, :], u, 0), part(RAW[:, u, :], u, 0), part(WHI[:, u, :], u, 0))\
                    .then_inc(first_lo, 1)

            split_first(0, 1)
            for k in range(KT):
                pool.wait_ge(xT_evac, k + 1)
                if k >= 2:
                    pool.wait_ge(p_ss, k - 1)
                pool.tensor_tensor(out=TP[:, k % 2, :], in0=XT[:, k, :], in1=XT[:, k, :], op=ALU.mult)\
                    .then_inc(p_sq, 1)
            split_first(1, 3)

            def ln_affine():
                pool.wait_ge(side_in, 16 * 6)
                pool.wait_ge(ln_scaled, 1)
                pool.tensor_tensor(out=GV[:, :, :], in0=GV[:, :, :], op=ALU.mult,
                                   in1=LNG[:, :].unsqueeze(1).to_broadcast([P, TB, T])).then_inc(pool_step, 1)
                pool.wait_ge(pool_step, 1)
                pool.tensor_tensor(out=GV[:, :, :], in0=GV[:, :, :], op=ALU.add,
                                   in1=LNB[:, :].unsqueeze(1).to_broadcast([P, TB, T])).then_inc(gv_ready, 1)

            def branch_lo(n):
                gi = GATE_JOBS.index(n)
                pool.wait_ge(br_hi, gi + 1)
                kind = KIND[n]
                ct = n - FIRST[(kind, 0)]
                if kind == "bg" and ct == 0:
                    pool.wait_ge(oc_done, 1)
                if kind == "cg" and ct == 0:
                    pool.wait_ge(oc_done, 2)
                sub(BRL[:, BRANCH[kind], ct, :], TT[:, gi % 2, :], BRH[:, BRANCH[kind], ct, :]).then_inc(br_lo, 1)

            def y_low(m):
                pool.wait_ge(y_hi, m + 1)
                sub(YL[:, m, :], TT[:, m % 2, :], YH[:, m, :]).then_inc(y_lo, 1)

            phase = {n: [] for n in range(NJ + 4)}
            phase[23].append((ln_affine,))
            for n in GATE_JOBS:
                phase[n + 2].append((branch_lo, n))
            for m in range(KT):
                phase[FIRST[("mix", 3 * (m // 2) + 2)] + 1 + m % 2].append((y_low, m))

            with pool.Fori(0, DEPTH) as layer:
                for n in range(NJ + 4):
                    if n < NJ and n > 0 and JOBS[n][1] == 0 and JOBS[n][0] + 1 < NU:
                        split_lo(JOBS[n][0] + 1)
                    for f, *a in phase[n]:
                        f(*a)
                split_first(0, 4 * layer + 5)
                split_first(1, 4 * layer + 7)
                pool.drain()
                pool.wait_ge(layer_done, 4)
                pool.sem_clear(range(first_num, last_num + 1))
                pool.sem_inc(layer_go, 1)

            pool.wait_ge(fg_in, 16)
            for i, n in enumerate(E_POOL):
                half, tb = divmod(n, TB)
                c = slice(half * T, (half + 1) * T)
                pool.wait_ge(e_scaled, i + 1)
                pool.tensor_tensor(out=OUT[:, tb, c], in0=OUT[:, tb, c], in1=FGB[:, c], op=ALU.mult)\
                    .then_inc(e_evac_pool, 1)

        @block.vector
        def _(dve):
            steps = [0]

            def chained(ins):
                steps[0] += 1
                ins.then_inc(vec_step, 1)
                dve.wait_ge(vec_step, steps[0])

            psteps = [0]

            def pchain(ins):
                psteps[0] += 1
                ins.then_inc(pro_step, 1)
                dve.wait_ge(pro_step, psteps[0])

            dve.wait_ge(pos_in, 16)
            dve.wait_ge(cst_in, 16)
            pchain(dve.tensor_copy(ANG[:, :], POSI[:, :]))
            pchain(dve.tensor_scalar(ANG[:, :], ANG[:, :], FREQ, None, ALU.mult))
            magic = 1.5 * 2.0 ** 23
            two_pi = 2.0 * np.pi
            c1 = 6.28125
            c2 = float(np.float32(np.round((two_pi - c1) * 2.0 ** 21) / 2.0 ** 21))
            c3 = float(np.float32(two_pi - c1 - c2))
            pchain(dve.tensor_scalar(TRN[:, :], ANG[:, :], float(1.0 / two_pi), magic, ALU.mult, ALU.add))
            pchain(dve.tensor_scalar(TRN[:, :], TRN[:, :], -magic, None, ALU.add))
            for c in (c1, c2, c3):
                pchain(dve.scalar_tensor_tensor(out=ANG[:, :], in0=TRN[:, :], scalar=-c, in1=ANG[:, :],
                                                op0=ALU.mult, op1=ALU.add))
            pchain(dve.tensor_scalar(ANG[:, :], ANG[:, :], 0.5, None, ALU.mult))
            dve.scalar_tensor_tensor(out=TRN[:, :], in0=ANG[:, :], scalar=-1.0, in1=ANG[:, :],
                                     op0=ALU.mult, op1=ALU.max).then_inc(p_half, 1)
            dve.wait_ge(vecT_done, 1)
            for c, cn, r0 in ((0, 8, 0), (8, 24, 16), (32, 4, 64)):
                last = dve.tensor_copy(VL[:, :, c:c + cn],
                                       M[0][:, r0:r0 + 2 * cn].rearrange("p (l c) -> p l c", l=2))
            last.then_inc(p_vec, 1)
            pchain(dve.tensor_copy(LBT[:, 24:32], M[0][:, 72:80]))
            dve.wait_ge(p_vec, 1)
            L0, L1, mx = LBT[:, 24:28], LBT[:, 28:32], LBT[:, 0:4]
            pchain(dve.tensor_tensor(out=mx, in0=L0, in1=L1, op=ALU.max))
            dve.tensor_tensor(out=LBT[:, 4:8], in0=L0, in1=mx, op=ALU.subtract)
            dve.tensor_tensor(out=LBT[:, 8:12], in0=L1, in1=mx, op=ALU.subtract).then_inc(p_diff, 1)

            def scaled_lo(k, layer, value):
                dve.wait_ge(xg_hi, value)
                return dve.scalar_tensor_tensor(out=HL[:, k, :], in0=XT[:, k, :], scalar=VL[:, layer, k:k + 1],
                                                in1=HH[:, k, :].bitcast(f32), op0=ALU.mult, op1=ALU.subtract)

            def split_first(u, value):
                dve.wait_ge(first_hi, value)
                dve.tensor_tensor(out=part(WLO[:, u, :], u, 1), in0=part(RAW[:, u, :], u, 1),
                                  in1=part(WHI[:, u, :], u, 1).bitcast(f32), op=ALU.subtract).then_inc(first_lo_vec, 1)

            def square_added(k):
                dve.wait_ge(p_sq, k + 1)
                if k == 0:
                    dve.tensor_copy(SS[:, :], TP[:, 0, :]).then_inc(p_ss, 1)
                    return
                dve.wait_ge(p_ss, k)
                add = dve.tensor_tensor(out=SS[:, :], in0=SS[:, :], in1=TP[:, k % 2, :], op=ALU.add)
                add.then_inc(ss_ready if k == KT - 1 else p_ss, 1)

            for k in range(KT):
                if k == 2:
                    split_first(0, 2)
                scaled_lo(k, 0, k + 1).then_inc(xg_lo, 1)
                if k >= 2:
                    square_added(k - 2)
            square_added(KT - 2)
            square_added(KT - 1)
            split_first(1, 4)
            dve.wait_ge(p_exp, 1)
            e0, e1, sm, p0, p1 = (LBT[:, c:c + 4] for c in (12, 16, 32, 36, 40))
            pchain(dve.tensor_tensor(out=sm, in0=e0, in1=e1, op=ALU.add))
            pchain(dve.reciprocal(sm, sm))
            pchain(dve.tensor_tensor(out=p0, in0=e0, in1=sm, op=ALU.mult))
            pchain(dve.tensor_tensor(out=p1, in0=e1, in1=sm, op=ALU.mult))
            pchain(dve.tensor_tensor(out=p1, in0=p0, in1=p1, op=ALU.add))
            pchain(dve.tensor_tensor(out=VL[:, 0, 36:40], in0=p0, in1=p0, op=ALU.subtract))
            pchain(dve.tensor_tensor(out=VL[:, 1, 36:40], in0=p1, in1=p0, op=ALU.subtract))
            pchain(dve.tensor_scalar(VL[:, :, 36:40], VL[:, :, 36:40], 0.0, 1.0, ALU.max, ALU.min))
            pchain(dve.tensor_scalar(VL[:, :, 40:44], VL[:, :, 36:40], -1.0, 1.0, ALU.mult, ALU.add))
            pchain(dve.tensor_scalar(VL[:, :, 44:48], VL[:, :, 40:44], -1.0, None, ALU.mult))
            dve.wait_ge(p_sin, 1)
            pchain(dve.tensor_tensor(out=SIN[:, :], in0=SH[:, :], in1=CH[:, :], op=ALU.mult))
            pchain(dve.tensor_scalar(SIN[:, :], SIN[:, :], SIGN2, None, ALU.mult))
            pchain(dve.tensor_tensor(out=COS[:, :], in0=SH[:, :], in1=SH[:, :], op=ALU.mult))
            dve.tensor_scalar(COS[:, :], COS[:, :], -2.0, 1.0, ALU.mult, ALU.add).then_inc(p_trig, 1)
            dve.wait_ge(p_trig, 1)

            def evac(n):
                u, t = JOBS[n]
                kind, i = UNITS[u]
                if kind not in BY_VECTOR:
                    return
                src = bank_of(n)[:, :]
                dve.wait_ge(pj_done, n + 1)
                if kind in ("cf", "cq"):
                    dst = (BC if kind == "cf" else QC)[i]
                    dve.tensor_tensor(out=dst[:, t, :], in0=src, in1=RS[:, :], op=ALU.mult).then_inc(vec_evac, 1)
                elif n in SG_JOBS:
                    s = SG_JOBS.index(n)
                    if s >= 2:
                        dve.wait_ge(gated, s - 1)
                    else:
                        dve.wait_ge(rope_done, 5)
                    dve.tensor_tensor(out=SG[:, s % 2, :], in0=src, in1=RS[:, :], op=ALU.mult).then_inc(vec_evac, 1)
                elif kind == "merge":
                    if i >= 2:
                        evacuated(dve, FIRST[("mix", i - 2)] + t)
                    dve.tensor_tensor(out=GM[:, i % 2, t, :], in0=src, in1=RS[:, :], op=ALU.mult)\
                       .then_inc(vec_evac, 1)
                elif kind == "mix":
                    p, b = divmod(i, 3)
                    dve.wait_ge(gm_ready, 2 * i + t + 1)
                    if b == 0:
                        if p == 0:
                            dve.wait_ge(br_lo, 12)
                            dve.wait_ge(oc_ready, 2)
                        else:
                            dve.wait_ge(y_lo, 2 * p)
                        dve.tensor_tensor(out=TT[:, t, :], in0=src, in1=GM[:, i % 2, t, :], op=ALU.mult)\
                           .then_inc(vec_evac, 1)
                        return
                    dve.tensor_tensor(out=TP[:, t, :], in0=src, in1=GM[:, i % 2, t, :], op=ALU.mult)\
                       .then_inc(vec_evac, 1)
                    evacuated(dve, n)
                    add = dve.tensor_tensor(out=TT[:, t, :], in0=TT[:, t, :], in1=TP[:, t, :], op=ALU.add)
                    if b == 2:
                        add.then_inc(y_full, 1)
                    else:
                        chained(add)
                else:
                    m = 2 * i + t
                    dve.tensor_tensor(out=XT[:, m, :], in0=src, in1=XT[:, m, :], op=ALU.add).then_inc(vec_evac, 1)

            def split_lo(u):
                dve.wait_ge(w_hi, 2 * (u - 1))
                dve.tensor_tensor(out=part(WLO[:, u % RB, :], u, 1), in0=part(RAW[:, u % RB, :], u, 1),
                                  in1=part(WHI[:, u % WB, :], u, 1).bitcast(f32), op=ALU.subtract).then_inc(w_lo_vec, 1)

            def rope(r):
                evacuated(dve, r)
                if r >= 1:
                    dve.wait_ge(rope_done, r)
                else:
                    dve.wait_ge(rstd_ready, 1)
                dst = QP[:, r, :] if r < 4 else KP[:, :]
                dve.tensor_tensor(out=R1[:, :], in0=QR[:, r % 3, :], in1=COS[:, :], op=ALU.mult)
                chained(dve.tensor_tensor(out=R2[:, :], in0=QS[:, r % 3, :], in1=SIN[:, :], op=ALU.mult))
                chained(dve.tensor_tensor(out=R1[:, :], in0=R1[:, :], in1=R2[:, :], op=ALU.add))
                dve.tensor_tensor(out=dst, in0=R1[:, :], in1=RS[:, :], op=ALU.mult).then_inc(rope_done, 1)

            def values_even():
                dve.wait_ge(va_ready, 1)
                dve.tensor_copy(VB[0:64, :, :], VA[0:64, :, :])
                dve.tensor_copy(VB[64:128, 1:TB, :], VA[64:128, 0:TB - 1, :]).then_inc(vb_ready, 1)

            def clamp(p):
                evacuated(dve, FIRST[("cf", p)] + 1)
                dve.tensor_scalar(BC[p][:, :, :], BC[p][:, :, :], -44.0, None, ALU.max).then_inc(clamped, 1)

            def neg_max(i):
                dve.wait_ge(scores_done, i + 1)
                chained(dve.memset(M[0][0:64, 64:128], MASK_VALUE))
                if i >= 1:
                    dve.wait_ge(negmax_ready, i)
                chained(dve.reduce_max(MX, M[0][:, :].rearrange("p (b k) -> p b k", b=TB), AX))
                if i >= 2:
                    dve.wait_ge(exp_done, i - 1)
                dve.tensor_scalar(NM[:, i % 2, :], MX, -SCALE, NSK[:, i:i + 1], ALU.mult, ALU.min)\
                   .then_inc(negmax_ready, 1)

            def normalise(i):
                dve.wait_ge(exp_done, i + 1)
                if i >= 1:
                    dve.wait_ge(probs_ready, i)
                chained(dve.tensor_tensor(out=DN, in0=SM[:, i % 2, :], in1=ES[:, i % 2, :], op=ALU.add))
                chained(dve.reciprocal(RD, DN))
                dve.tensor_tensor(out=PR[:, i % 2, :, :], in0=PR[:, i % 2, :, :],
                                  in1=RD.unsqueeze(2).to_broadcast([P, TB, P]), op=ALU.mult).then_inc(probs_ready, 1)

            def attn_out(j):
                dve.wait_ge(pv_done, 2 * j + 2)
                dve.tensor_copy(OX[:, 0, j, :], M[2][:, :]).then_inc(oa_evac, 1)

            def keys_and_sums(p):
                dve.wait_ge(logf_ready, p + 1)
                for hh in range(2):
                    h = 2 * p + hh
                    dve.tensor_scalar(KK[p][:, hh, :], KK[p][:, hh, :], noml[:, h:h + 1], oml[:, h:h + 1],
                                      ALU.mult, ALU.add)
                for hh in range(2):
                    for tb in range(TB):
                        b = BC[p][:, hh, tb * P:(tb + 1) * P]
                        last = dve.tensor_tensor_scan(b, ONE[:, :], b, 0.0, ALU.mult, ALU.add)
                last.then_inc(c_keys, 1)
                dve.wait_ge(c_keys, p + 1)

            def halves(a, s):
                return a.rearrange("p (b u s) -> p b u s", u=2, s=s)

            def diffs(p, lev):
                s = 64 >> lev
                b = halves(BC[p][:, :, :].rearrange("p h t -> p (h t)"), s)
                e = halves(E[lev % 2][:, :], s)
                if (p, lev) == (0, 0):
                    dve.wait_ge(rope_done, 5)
                elif lev >= 2:
                    dve.wait_ge(ops_ready, LEVELS * p + lev - 1)
                elif p == 1:
                    dve.wait_ge(state_ready, 1)
                mid = b[:, :, 0, s - 1:s].to_broadcast([P, 1024 // (2 * s), s])
                dve.tensor_tensor(out=e[:, :, 0, :], in0=mid, in1=b[:, :, 0, :], op=ALU.subtract)
                dve.tensor_tensor(out=e[:, :, 1, :], in0=b[:, :, 1, :], in1=mid, op=ALU.subtract).then_inc(diff_done, 1)

            def operands(p, lev):
                s = 64 >> lev
                n = LEVELS * p + lev
                dve.wait_ge(decay_ready, (LEVELS + 1) * p + lev + 1)
                if n >= 2:
                    q, back = divmod(n - 2, LEVELS)
                    dve.wait_ge(lev_done, (LEVELS + 1) * q + back + 2)
                e, o = halves(E[lev % 2][:, :], s), halves(XL[lev % 2][:, :], s)
                k, q = (halves(a[p][:, :, :].rearrange("p h t -> p (h t)"), s) for a in (KK, QC))
                dve.tensor_tensor(out=o[:, :, 0, :], in0=k[:, :, 0, :], in1=e[:, :, 0, :], op=ALU.mult)
                if lev == 0:
                    evacuated(dve, FIRST[("cq", p)] + 1)
                dve.tensor_tensor(out=o[:, :, 1, :], in0=q[:, :, 1, :], in1=e[:, :, 1, :], op=ALU.mult)\
                   .then_inc(ops_ready, 1)

            def take_diagonal(p):
                dve.wait_ge(lev_done, (LEVELS + 1) * p + 1)
                if p == 0:
                    dve.wait_ge(rope_done, 5)
                else:
                    dve.wait_ge(oc_ready, 1)
                for hh in range(2):
                    last = dve.tensor_tensor(out=AT[:, hh, :].rearrange("p (b t) -> p b t", b=TB),
                                             in0=M[3 + hh][:, :].rearrange("p (b t) -> p b t", b=TB),
                                             in1=ID.unsqueeze(1).to_broadcast([P, TB, P]), op=ALU.mult)
                last.then_inc(at_evac, 1)

            def take_level(p, lev):
                s = 64 >> lev
                dve.wait_ge(lev_done, (LEVELS + 1) * p + lev + 2)
                dve.wait_ge(at_evac, (LEVELS + 1) * p + lev + 1)
                dst = AT[:, :, :].rearrange("p h (b u s) -> p (h b) u s", u=2, s=s)[:, :, 1, :]
                nb = 64 // s
                src = M[3 + lev % 2][:, :].rearrange("p (c b s) -> p c b s", b=nb, s=s)
                dst = dst.rearrange("p (c b) s -> p c b s", b=nb)
                if lev == 0:
                    dve.tensor_copy(dst[0:64], src[0:64]).then_inc(at_evac, 1)
                    return
                msk = mask(lev).rearrange("p (b s) -> p b s", s=s).unsqueeze(1).to_broadcast([P, 2 * TB, nb, s])
                dve.copy_predicated(dst, msk, src).then_inc(at_evac, 1)

            def block_diffs(p):
                b = BC[p][:, :, :].rearrange("p h (c t) -> p h c t", t=P)
                dve.wait_ge(ops_ready, LEVELS * (p + 1) - 1)
                for hh in range(2):
                    last = dve.tensor_tensor(out=E[1][:, hh * 3 * P:(hh + 1) * 3 * P].rearrange("p (c t) -> p c t", t=P),
                                             in0=b[:, hh, 0:3, P - 1:P].to_broadcast([P, 3, P]),
                                             in1=b[:, hh, 0:3, :], op=ALU.subtract)
                last.then_inc(diff_done, 1)

            def decayed(p):
                dve.wait_ge(decay_ready, (LEVELS + 1) * (p + 1))
                dve.wait_ge(lev_done, (LEVELS + 1) * p + 1)
                dve.wait_ge(ops_ready, LEVELS * (p + 1))
                for hh in range(2):
                    dve.tensor_tensor(out=KK[p][:, hh, 0:3 * P], in0=KK[p][:, hh, 0:3 * P],
                                      in1=E[1][:, hh * 3 * P:(hh + 1) * 3 * P], op=ALU.mult)
                dve.tensor_tensor(out=QC[p][:, :, :].rearrange("p h t -> p (h t)"),
                                  in0=QC[p][:, :, :].rearrange("p h t -> p (h t)"), in1=E[0][:, :], op=ALU.mult)\
                   .then_inc(khat_ready, 1)

            def states(p):
                dve.wait_ge(upd_done, p + 1)
                if p == 1:
                    dve.wait_ge(oc_done, 1)
                for hh in range(2):
                    chained(dve.tensor_copy(ST[:, hh, 0, :], M[3 + hh][:, 0:P]))
                for c in (1, 2):
                    for hh in range(2):
                        eb = E[0][:, hh * T + (c + 1) * P - 1:hh * T + (c + 1) * P]
                        last = dve.scalar_tensor_tensor(out=ST[:, hh, c, :], in0=ST[:, hh, c - 1, :], scalar=eb,
                                                        in1=M[3 + hh][:, c * P:(c + 1) * P],
                                                        op0=ALU.mult, op1=ALU.add)
                        if (c, hh) != (2, 1):
                            chained(last)
                last.then_inc(state_ready, 1)

            def head_scaled(p):
                dve.wait_ge(oc_rstd, p + 1)
                for hh in range(2):
                    h = 2 * p + hh
                    last = dve.scalar_tensor_tensor(out=OX[:, 2, h, :], in0=OX[:, 2, h, :], scalar=hng[:, h:h + 1],
                                                    in1=AT[:, hh, :], op0=ALU.mult, op1=ALU.mult)
                last.then_inc(oc_ready, 1)

            def spatial_mask():
                dve.wait_ge(wT_evac, 1)
                dve.memset(WT[64:128, :, 0:64], 0.0).then_inc(wT_ready, 1)

            def layer_norm_stats():
                evacuated(dve, FIRST[("bv", 1)] + 1)
                for tb in range(TB):
                    last = dve.bn_stats(BS[:, tb, :], GV[:, tb, :])
                chained(last)
                for tb in range(TB):
                    last = dve.bn_aggr(MV[:, tb, :], BS[:, tb, :])
                last.then_inc(ln_stats, 1)

            def layer_norm_scale():
                dve.wait_ge(ln_rstd, 1)
                for tb in range(TB):
                    last = dve.tensor_scalar(GV[:, tb, :], GV[:, tb, :], MV[:, tb, 0:1], RL[:, tb:tb + 1],
                                             ALU.subtract, ALU.mult)
                last.then_inc(ln_scaled, 1)

            def gate_product(n):
                s = SG_JOBS.index(n)
                kind = KIND[n]
                ct = n - FIRST[(kind, 0)]
                if kind == "bu":
                    dve.wait_ge(sv_done, ct + 1)
                    chained(dve.tensor_tensor(out=OX[:, 1, ct, :].rearrange("p (n t) -> p n t", t=P),
                                              in0=M[ct % 3][:, :].rearrange("p (n t) -> p n t", t=P),
                                              in1=SPB[:, ct, :].unsqueeze(1).to_broadcast([P, TB, P]), op=ALU.add))
                    dve.wait_ge(sg_ready, s + 1)
                    dve.tensor_tensor(out=OX[:, 1, ct, :], in0=OX[:, 1, ct, :], in1=SG[:, s % 2, :], op=ALU.mult)\
                       .then_inc(gated, 1)
                    return
                gi = GATE_JOBS.index(n)
                if gi >= 2:
                    dve.wait_ge(br_lo, gi - 1)
                br = BRANCH[kind]
                if kind == "ag":
                    dve.wait_ge(oa_evac, ct + 1)
                if kind == "bg":
                    dve.wait_ge(gated, SG_JOBS.index(FIRST[("bu", 0)] + ct) + 1)
                if kind == "cg":
                    dve.wait_ge(oc_ready, ct // 2 + 1)
                dve.wait_ge(sg_ready, s + 1)
                dve.tensor_tensor(out=TT[:, gi % 2, :], in0=OX[:, br, ct, :], in1=SG[:, s % 2, :], op=ALU.mult)\
                   .then_inc(gated, 1)

            def next_x(m, layer):
                dve.wait_ge(sq_ready, m + 1)
                if m == 0:
                    dve.wait_ge(state_ready, 2)
                    dve.tensor_copy(SS[:, :], TP[:, 0, :]).then_inc(ss_added, 1)
                else:
                    dve.wait_ge(ss_added, m)
                    add = dve.tensor_tensor(out=SS[:, :], in0=SS[:, :], in1=TP[:, m % 2, :], op=ALU.add)
                    add.then_inc(ss_ready if m == KT - 1 else ss_added, 1)
                scaled_lo(m, DEPTH - 1, (layer + 1) * KT + m + 1).then_inc(xg_lo, 1)

            def sinks():
                dve.wait_ge(side_in, 16 * 6)
                chained(dve.tensor_scalar(NSK, SK, -1.0, None, ALU.mult))

            phase = {n: [] for n in range(NJ + 4)}
            for r, n in enumerate(ROPE_AT):
                phase[n].append((rope, r))
            phase[6].append((sinks,))
            phase[FIRST[("v", 0)] + 4].append((values_even,))
            for i in range(A_HEADS):
                phase[8 + i].append((neg_max, i))
            for p, d in enumerate(DIAG):
                phase[FIRST[("cf", p)] + 2].append((clamp, p))
                phase[FIRST[("cf", p)] + 3].append((keys_and_sums, p))
                phase[d - 1].append((diffs, p, 0))
                phase[d + 1].append((take_diagonal, p))
                for lev in range(LEVELS):
                    if lev + 1 < LEVELS:
                        phase[d + lev].append((diffs, p, lev + 1))
                    phase[d + lev].append((operands, p, lev))
                    phase[d + lev + 2].append((take_level, p, lev))
                phase[d + LEVELS - 1].append((block_diffs, p))
                phase[d + LEVELS].append((decayed, p))
                phase[d + LEVELS + 3].append((states, p))
                phase[d + LEVELS + 5].append((head_scaled, p))
            for i in range(A_HEADS):
                phase[8 + i].append((normalise, i))
            for j in range(4):
                phase[12 + 2 * j].append((attn_out, j))
            phase[20].append((spatial_mask,))
            phase[22].append((layer_norm_stats,))
            phase[22].append((layer_norm_scale,))
            for n in SG_JOBS:
                phase[n + 2].append((gate_product, n))
            for m in range(KT):
                phase[FIRST[("out", 0)] + m + 1].append((next_x, m, "layer"))

            with dve.Fori(0, DEPTH) as layer:
                dve.wait_ge(layer_go, layer + 1)
                steps[0] = 0
                dve.tensor_copy(VC48, VL[:, layer, :]).then_inc(vecs_ready, 1)
                dve.memset(VB[64:128, 0, :], 0.0).then_inc(first_zero, 1)
                dve.wait_ge(vecs_ready, 1)
                for n in range(NJ + 4):
                    split = n < NJ and n > 0 and JOBS[n][1] == 0 and JOBS[n][0] + 1 < NU
                    early = n <= FIRST[("cf", 0)] or n < NJ and JOBS[n][0] >= UNITS.index(("merge", 0)) - 1
                    if split and early:
                        split_lo(JOBS[n][0] + 1)
                    for f, *a in phase[n]:
                        f(*[layer if v == "layer" else v for v in a])
                    if split and not early:
                        split_lo(JOBS[n][0] + 1)
                    if n == JOBS_TO[NU - 2] + 1:
                        split_first(0, 4 * layer + 6)
                    if n < NJ:
                        evac(n)
                split_first(1, 4 * layer + 8)
                dve.drain().then_inc(layer_done, 1)

            dve.wait_ge(p_act, 1)
            dve.reciprocal(RT, RT).then_inc(e_rstd, 1)
            dve.wait_ge(e_rstd, 1)
            dve.wait_ge(fg_in, 16)
            for n in E_VEC:
                half, tb = divmod(n, TB)
                dve.wait_ge(e_tr, n + 1)
                dve.scalar_tensor_tensor(out=OUT[:, tb, half * T:(half + 1) * T], in0=out_bank(n)[:, :],
                                         scalar=RT[:, tb:tb + 1], in1=FGB[:, half * T:(half + 1) * T],
                                         op0=ALU.mult, op1=ALU.mult).then_inc(e_evac, 1)


_INS = ["x", "positions", "w_in", "b_merge", "w_branch", "w_out", "norm_g", "final_g", "attn_sinks", "sp_w",
        "sp_b", "sp_ln_g", "sp_ln_b", "hgrn_lb", "hgrn_norm_g"]


def kernel(**inputs):
    import numpy as _np
    import concourse.bacc as _bacc
    from concourse import mybir as _mybir
    from concourse.bass_utils import run_bass_kernel_spmd as _run

    nc = _bacc.Bacc("TRN2", target_bir_lowering=False, num_devices=1)
    arrays = {f"in_{n}": _np.ascontiguousarray(inputs[n]) for n in _INS}
    arrays["in_consts"] = constants()
    args = {n[3:]: nc.dram_tensor(n, a.shape, _mybir.dt.from_np(a.dtype), kind="ExternalInput").ap()
            for n, a in arrays.items()}
    o = nc.dram_tensor("out_0", (1, T, D), _mybir.dt.float32, kind="ExternalOutput").ap()
    build(nc, out=o, **args)
    return _run(nc, [arrays], core_ids=[0]).results[0]["out_0"]
```
